# Optimizing a Trainium2 kernel written in Bass

```python
import jax, jax.numpy as jnp
from jax import lax
import numpy as np

D_MODEL = 1024
BATCH = 1
SEQ = 512
DEPTH = 2

N_HEADS = 16
N_KV_HEADS = 2
HEAD_DIM = 64
GROUP = N_HEADS // N_KV_HEADS
ROT_DIM = HEAD_DIM // 4
ROPE_THETA = 500000.0
WINDOW = 128
BLOCK = 128
CONV_CH = D_MODEL // 2
CONV_WIDTH = 31
D_FF = -(-(8 * D_MODEL) // (3 * 256)) * 256
EPS = 1e-6
Q_W = N_HEADS * HEAD_DIM
KV_W = N_KV_HEADS * HEAD_DIM
IN_W = Q_W + 2 * KV_W + 2 * CONV_CH + 2 * D_MODEL
SPLITS = tuple(int(s) for s in np.cumsum([Q_W, KV_W, KV_W, CONV_CH, CONV_CH, D_MODEL])[:])


def rmsnorm(x, g):
    xf = x.astype(jnp.float32)
    y = xf * lax.rsqrt(jnp.mean(xf * xf, axis=-1, keepdims=True) + EPS)
    return (y * g.astype(jnp.float32)).astype(x.dtype)

def layernorm(x, g, b):
    xf = x.astype(jnp.float32)
    mu = jnp.mean(xf, axis=-1, keepdims=True)
    var = jnp.mean(jnp.square(xf - mu), axis=-1, keepdims=True)
    y = (xf - mu) * lax.rsqrt(var + EPS)
    return (y * g.astype(jnp.float32) + b.astype(jnp.float32)).astype(x.dtype)

def rope_tables(seq):
    inv_freq = ROPE_THETA ** (-jnp.arange(0, ROT_DIM, 2, dtype=jnp.float32) / ROT_DIM)
    ang = jnp.arange(seq, dtype=jnp.float32)[:, None] * inv_freq[None, :]
    return jnp.cos(ang), jnp.sin(ang)

def partial_rope(x, cos, sin):
    half = ROT_DIM // 2
    c = cos[None, :, None, :].astype(x.dtype)
    s = sin[None, :, None, :].astype(x.dtype)
    x1, x2, xp = x[..., :half], x[..., half:ROT_DIM], x[..., ROT_DIM:]
    return jnp.concatenate([x1 * c - x2 * s, x2 * c + x1 * s, xp], axis=-1)

def sliding_window_attention(q, k, v, sinks):
    B, T = q.shape[0], q.shape[1]
    nb = T // BLOCK
    qb = q.reshape(B, nb, BLOCK, N_KV_HEADS, GROUP, HEAD_DIM)

    def band(t):
        tp = jnp.pad(t, ((0, 0), (BLOCK, 0), (0, 0), (0, 0)))
        tp = tp.reshape(B, nb + 1, BLOCK, N_KV_HEADS, HEAD_DIM)
        return jnp.concatenate([tp[:, :-1], tp[:, 1:]], axis=2)

    kb, vb = band(k), band(v)
    scale = HEAD_DIM ** -0.5
    s = jnp.einsum('bnqkgd,bnskd->bnkgqs', qb, kb,
                   preferred_element_type=jnp.float32) * scale
    qi = jnp.arange(BLOCK)[:, None]
    sj = jnp.arange(2 * BLOCK)[None, :]
    rel = qi + BLOCK - sj
    kpos = jnp.arange(nb)[:, None, None] * BLOCK - BLOCK + sj
    mask = (rel >= 0) & (rel < WINDOW) & (kpos >= 0)
    s = jnp.where(mask[None, :, None, None], s, -jnp.inf)
    sink = sinks.astype(jnp.float32).reshape(N_KV_HEADS, GROUP)[None, None, :, :, None, None]
    m = jnp.maximum(jnp.max(s, axis=-1, keepdims=True), sink)
    p = jnp.exp(s - m)
    p = p / (jnp.sum(p, axis=-1, keepdims=True) + jnp.exp(sink - m))
    o = jnp.einsum('bnkgqs,bnskd->bnqkgd', p.astype(v.dtype), vb)
    return o.reshape(B, T, N_HEADS * HEAD_DIM)

def conformer_conv(u, ug, w_dw, b_dw, ln_g, ln_b, w_pw):
    a = u * jax.nn.sigmoid(ug)
    y = lax.conv_general_dilated(
        a, w_dw[:, None, :].astype(a.dtype), window_strides=(1,),
        padding=[(CONV_WIDTH - 1, 0)],
        dimension_numbers=('NWC', 'WIO', 'NWC'),
        feature_group_count=CONV_CH) + b_dw.astype(a.dtype)
    y = layernorm(y, ln_g, ln_b)
    y = jax.nn.silu(y)
    return jnp.einsum('btc,cd->btd', y, w_pw)

def first_inputs(seed: int = 0) -> dict:
    key = jax.random.key(seed)
    ks = jax.random.split(key, 16)
    f32 = jnp.float32

    def nrm(k, shape, scale):
        return jax.random.normal(k, shape, f32) * scale

    return {
        "x": nrm(ks[0], (BATCH, SEQ, D_MODEL), 1.0),
        "norm_mix": 1.0 + nrm(ks[1], (DEPTH, D_MODEL), 0.02),
        "w_in": nrm(ks[2], (DEPTH, D_MODEL, IN_W), D_MODEL ** -0.5),
        "q_norm": 1.0 + nrm(ks[3], (DEPTH, HEAD_DIM), 0.02),
        "k_norm": 1.0 + nrm(ks[4], (DEPTH, HEAD_DIM), 0.02),
        "sinks": nrm(ks[5], (DEPTH, N_HEADS), 0.5),
        "conv_w": nrm(ks[6], (DEPTH, CONV_WIDTH, CONV_CH), CONV_WIDTH ** -0.5),
        "conv_b": nrm(ks[7], (DEPTH, CONV_CH), 0.02),
        "conv_ln_g": 1.0 + nrm(ks[8], (DEPTH, CONV_CH), 0.02),
        "conv_ln_b": nrm(ks[9], (DEPTH, CONV_CH), 0.02),
        "w_conv_out": nrm(ks[10], (DEPTH, CONV_CH, D_MODEL), CONV_CH ** -0.5),
        "w_out": nrm(ks[11], (DEPTH, D_MODEL, D_MODEL), D_MODEL ** -0.5),
        "norm_ffn": 1.0 + nrm(ks[12], (DEPTH, D_MODEL), 0.02),
        "w_gate_up": nrm(ks[13], (DEPTH, D_MODEL, 2 * D_FF), D_MODEL ** -0.5),
        "w_down": nrm(ks[14], (DEPTH, D_FF, D_MODEL), D_FF ** -0.5),
    }

def first_block(x, norm_mix, w_in, q_norm, k_norm, sinks, conv_w, conv_b, conv_ln_g,
              conv_ln_b, w_conv_out, w_out, norm_ffn, w_gate_up, w_down):
    B, T = x.shape[0], x.shape[1]
    cos, sin = rope_tables(T)
    for l in range(DEPTH):
        h = rmsnorm(x, norm_mix[l])
        proj = jnp.einsum('btd,de->bte', h, w_in[l])
        q, k, v, u, ug, ga, gb = jnp.split(proj, SPLITS, axis=-1)
        q = q.reshape(B, T, N_HEADS, HEAD_DIM)
        k = k.reshape(B, T, N_KV_HEADS, HEAD_DIM)
        v = v.reshape(B, T, N_KV_HEADS, HEAD_DIM)
        q = partial_rope(rmsnorm(q, q_norm[l]), cos, sin)
        k = partial_rope(rmsnorm(k, k_norm[l]), cos, sin)
        a_out = sliding_window_attention(q, k, v, sinks[l])
        c_out = conformer_conv(u, ug, conv_w[l], conv_b[l], conv_ln_g[l],
                               conv_ln_b[l], w_conv_out[l])
        merged = jax.nn.sigmoid(ga) * a_out + jax.nn.sigmoid(gb) * c_out
        x = x + jnp.einsum('btd,de->bte', merged, w_out[l])
        h2 = rmsnorm(x, norm_ffn[l])
        gu = jnp.einsum('btd,df->btf', h2, w_gate_up[l])
        g, up = jnp.split(gu, 2, axis=-1)
        x = x + jnp.einsum('btf,fd->btd', jax.nn.silu(g) * up, w_down[l])
    return x


DEPTH_2 = 1

CHUNK = 128
RET_HEADS = 4
RET_DK = 128
RET_DV = 256
RET_QK_W = RET_HEADS * RET_DK
RET_V_W = RET_HEADS * RET_DV
SGU_GROUPS = 4
SGU_W = 1024
SGU_GW = SGU_W // SGU_GROUPS
D_FF_2 = 2816
CONV_W = 3
ROPE_BASE = 10000.0
IN_SPLITS = (RET_QK_W, RET_QK_W, RET_V_W, RET_V_W, SGU_W, SGU_W, D_MODEL, D_MODEL)
IN_W_2 = sum(IN_SPLITS)


def _rmsnorm(x, g):
    xf = x.astype(jnp.float32)
    y = xf * lax.rsqrt(jnp.mean(xf * xf, axis=-1, keepdims=True) + EPS)
    return (y * g.astype(jnp.float32)).astype(x.dtype)

def _layernorm(x, g=None, b=None):
    xf = x.astype(jnp.float32)
    mu = jnp.mean(xf, axis=-1, keepdims=True)
    var = jnp.mean(jnp.square(xf - mu), axis=-1, keepdims=True)
    y = (xf - mu) * lax.rsqrt(var + EPS)
    if g is not None:
        y = y * g.astype(jnp.float32) + b.astype(jnp.float32)
    return y.astype(x.dtype)

def _rotary(t):
    S, d = t.shape[1], t.shape[-1]
    half = d // 2
    inv_freq = 1.0 / (ROPE_BASE ** (jnp.arange(half, dtype=jnp.float32) / half))
    ang = jnp.arange(S, dtype=jnp.float32)[:, None] * inv_freq[None, :]
    cos = jnp.cos(ang)[None, :, None, :].astype(t.dtype)
    sin = jnp.sin(ang)[None, :, None, :].astype(t.dtype)
    t1, t2 = t[..., :half], t[..., half:]
    return jnp.concatenate([t1 * cos - t2 * sin, t1 * sin + t2 * cos], axis=-1)

def _to_chunks(t):
    B, S, H, d = t.shape
    return t.reshape(B, S // CHUNK, CHUNK, H, d).transpose(0, 3, 1, 2, 4)

def _from_chunks(t):
    B, H, N, C, d = t.shape
    return t.transpose(0, 2, 3, 1, 4).reshape(B, N * C, H, d)

def _retention_one_direction(q, k, v, log_gamma, strict):
    dt = q.dtype
    idx = jnp.arange(CHUNK, dtype=jnp.float32)
    diff = idx[:, None] - idx[None, :]
    mask = (diff > 0) if strict else (diff >= 0)
    lg = log_gamma[:, None, None]
    dmat = jnp.where(mask[None], jnp.exp(jnp.where(mask, diff, 0.0)[None] * lg), 0.0)
    s = jnp.einsum('bhncd,bhnmd->bhncm', q, k) * dmat[None, :, None].astype(dt)
    intra = jnp.einsum('bhncm,bhnme->bhnce', s, v)
    zeta = jnp.exp((CHUNK - 1.0 - idx)[None, :] * log_gamma[:, None]).astype(dt)
    xi = jnp.exp((idx + 1.0)[None, :] * log_gamma[:, None]).astype(dt)
    decay_c = jnp.exp(CHUNK * log_gamma).astype(dt)[None, :, None, None]
    kv = jnp.einsum('bhnmd,bhnme->nbhde', k, v * zeta[None, :, None, :, None])

    def step(state, kv_n):
        return decay_c * state + kv_n, state

    _, r_prev = lax.scan(step, jnp.zeros_like(kv[0]), kv)
    cross = jnp.einsum('bhncd,nbhde->bhnce', q * xi[None, :, None, :, None], r_prev)
    return intra + cross

def _retention_branch(q, k, v, g, ret_decay_logit, w_ret_o):
    B, S, _ = q.shape
    q = _rotary(q.reshape(B, S, RET_HEADS, RET_DK))
    k = _rotary(k.reshape(B, S, RET_HEADS, RET_DK)) * (RET_DK ** -0.5)
    v = v.reshape(B, S, RET_HEADS, RET_DV)
    log_gamma = jax.nn.log_sigmoid(ret_decay_logit.astype(jnp.float32))
    fwd = _retention_one_direction(_to_chunks(q), _to_chunks(k), _to_chunks(v), log_gamma[0], False)
    qb, kb, vb = (jnp.flip(t, axis=1) for t in (q, k, v))
    bwd = _retention_one_direction(_to_chunks(qb), _to_chunks(kb), _to_chunks(vb), log_gamma[1], True)
    o = _from_chunks(fwd) + jnp.flip(_from_chunks(bwd), axis=1)
    o = _layernorm(o).reshape(B, S, RET_V_W)
    return (o * jax.nn.silu(g)) @ w_ret_o

def _sgu_branch(u, sv, sgu_ln_g, sgu_ln_b, w_spatial, b_spatial, w_sgu_o):
    B, S, _ = u.shape
    u = jax.nn.gelu(u)
    sv = _layernorm(jax.nn.gelu(sv), sgu_ln_g, sgu_ln_b)
    svc = sv.reshape(B, S // CHUNK, CHUNK, SGU_GROUPS, SGU_GW)
    mixed = jnp.einsum('gpq,bnqgc->bnpgc', w_spatial, svc) + b_spatial.T[None, None, :, :, None]
    y = u * mixed.reshape(B, S, SGU_W)
    return y @ w_sgu_o

def _conv_gated_mlp(h, w_up, conv_w, conv_b, w_down):
    hid = h @ w_up
    c = hid.shape[-1]
    hid = lax.conv_general_dilated(
        hid, conv_w.reshape(CONV_W, 1, c), window_strides=(1,),
        padding=((CONV_W // 2, CONV_W // 2),),
        dimension_numbers=('NWC', 'WIO', 'NWC'), feature_group_count=c) + conv_b
    a, b = jnp.split(hid, 2, axis=-1)
    return (jax.nn.gelu(a) * b) @ w_down

def second_inputs(seed: int = 0) -> dict:
    key = jax.random.key(seed)
    ks = jax.random.split(key, 20)
    f32 = jnp.float32
    nrm = lambda k, shape, s: jax.random.normal(k, shape, f32) * s
    gamma0 = 1.0 - 2.0 ** (-5.0 - np.arange(RET_HEADS, dtype=np.float32))
    logit0 = jnp.asarray(np.log(gamma0) - np.log1p(-gamma0), f32)
    return {
        "x": nrm(ks[0], (BATCH, SEQ, D_MODEL), 1.0),
        "g_pre_mix": 1.0 + nrm(ks[1], (D_MODEL,), 0.05),
        "w_in": nrm(ks[2], (D_MODEL, IN_W_2), D_MODEL ** -0.5),
        "ret_decay_logit": logit0[None, :] + nrm(ks[3], (2, RET_HEADS), 0.1),
        "sgu_ln_g": 1.0 + nrm(ks[4], (SGU_W,), 0.05),
        "sgu_ln_b": nrm(ks[5], (SGU_W,), 0.02),
        "w_spatial": nrm(ks[6], (SGU_GROUPS, CHUNK, CHUNK), CHUNK ** -0.5),
        "b_spatial": nrm(ks[7], (SGU_GROUPS, CHUNK), 0.02),
        "w_ret_o": nrm(ks[8], (RET_V_W, D_MODEL), RET_V_W ** -0.5),
        "w_sgu_o": nrm(ks[9], (SGU_W, D_MODEL), SGU_W ** -0.5),
        "w_out": nrm(ks[10], (D_MODEL, D_MODEL), D_MODEL ** -0.5),
        "g_post_mix": 1.0 + nrm(ks[11], (D_MODEL,), 0.05),
        "g_pre_ffn": 1.0 + nrm(ks[12], (D_MODEL,), 0.05),
        "w_up": nrm(ks[13], (D_MODEL, 2 * D_FF_2), D_MODEL ** -0.5),
        "conv_w": nrm(ks[14], (CONV_W, 2 * D_FF_2), CONV_W ** -0.5),
        "conv_b": nrm(ks[15], (2 * D_FF_2,), 0.02),
        "w_down": nrm(ks[16], (D_FF_2, D_MODEL), D_FF_2 ** -0.5),
        "g_post_ffn": 1.0 + nrm(ks[17], (D_MODEL,), 0.05),
    }

def second_block(x, g_pre_mix, w_in, ret_decay_logit, sgu_ln_g, sgu_ln_b, w_spatial, b_spatial,
              w_ret_o, w_sgu_o, w_out, g_post_mix, g_pre_ffn, w_up, conv_w, conv_b, w_down,
              g_post_ffn):
    for _ in range(DEPTH_2):
        h = _rmsnorm(x, g_pre_mix)
        proj = h @ w_in
        q, k, v, g, u, sv, a_ret, a_sgu = jnp.split(proj, list(np.cumsum(IN_SPLITS)[:-1]), axis=-1)
        y_ret = _retention_branch(q, k, v, g, ret_decay_logit, w_ret_o)
        y_sgu = _sgu_branch(u, sv, sgu_ln_g, sgu_ln_b, w_spatial, b_spatial, w_sgu_o)
        merged = jax.nn.sigmoid(a_ret) * y_ret + jax.nn.sigmoid(a_sgu) * y_sgu
        x = x + _rmsnorm(merged @ w_out, g_post_mix)
        h2 = _rmsnorm(x, g_pre_ffn)
        x = x + _rmsnorm(_conv_gated_mlp(h2, w_up, conv_w, conv_b, w_down), g_post_ffn)
    return x


def setup_inputs(seed=0):
    out = dict(first_inputs(seed))
    for name, value in second_inputs(seed + 1).items():
        if name != "x":
            out[name + "_2"] = value
    return out


def reference(
    x, norm_mix, w_in, q_norm, k_norm, sinks, conv_w, conv_b, conv_ln_g, conv_ln_b, w_conv_out,
    w_out, norm_ffn, w_gate_up, w_down, g_pre_mix_2, w_in_2, ret_decay_logit_2, sgu_ln_g_2,
    sgu_ln_b_2, w_spatial_2, b_spatial_2, w_ret_o_2, w_sgu_o_2, w_out_2, g_post_mix_2,
    g_pre_ffn_2, w_up_2, conv_w_2, conv_b_2, w_down_2, g_post_ffn_2,
):
    x = first_block(
        x, norm_mix, w_in, q_norm, k_norm, sinks, conv_w, conv_b, conv_ln_g, conv_ln_b,
        w_conv_out, w_out, norm_ffn, w_gate_up, w_down,
    )
    return second_block(
        x, g_pre_mix_2, w_in_2, ret_decay_logit_2, sgu_ln_g_2, sgu_ln_b_2, w_spatial_2,
        b_spatial_2, w_ret_o_2, w_sgu_o_2, w_out_2, g_post_mix_2, g_pre_ffn_2, w_up_2, conv_w_2,
        conv_b_2, w_down_2, g_post_ffn_2,
    )


_drawn_inputs = setup_inputs


def setup_inputs(seed=0):
    import zlib

    import numpy as np

    out = dict(_drawn_inputs(seed))
    spreads = {}
    factors = {'norm_mix': 3.009,
     'q_norm': 8.0,
     'k_norm': 8.0,
     'sinks': 18.089,
     'conv_ln_g': 3.41,
     'conv_ln_b': 3.681,
     'sgu_ln_b_2': 20.338,
     'b_spatial_2': 19.359,
     'conv_b_2': 4.06,
     'sgu_ln_g_2': 5.611,
     'g_post_mix_2': 3.79,
     'g_pre_ffn_2': 3.029,
     'g_post_ffn_2': 4.334}
    for name, (base, spread) in spreads.items():
        noise = np.random.default_rng([zlib.crc32(name.encode()), seed]).standard_normal(out[name].shape)
        drawn = base * np.exp(spread * noise) if base else spread * noise
        out[name] = __import__('jax').numpy.asarray(drawn.astype(out[name].dtype))
    for name, factor in factors.items():
        out[name] = (out[name] * factor).astype(out[name].dtype)
    return out
```

```python
from contextlib import ExitStack, contextmanager

import concourse.bass as bass
from concourse import mybir
import numpy as np

ALU = mybir.AluOpType
ACT = mybir.ActivationFunctionType
F32 = mybir.dt.float32
F32R = mybir.dt.float32r
AX_X = mybir.AxisListType.X

P = 128
D = 1024
T = 512
KT = D // P
TB = T // P
DEPTH = 2
HEADS, KV_HEADS, HD = 16, 2, 64
QT = HEADS * HD // P
CONV_CH, TAPS = 512, 31
CT = CONV_CH // P
PADW = T + TAPS - 1
FF = 2816
FT = FF // P
EPS = 1e-6
ROT = HD // 4
RH, DK, DV = 4, 128, 256
SGU_G = 4
DWIN = T + (TB - 1) * P
CH = 2048
HALF = FT // 2 * P

L_UG, L_K, L_V, L_QG, L_GC, L_OUT, L_GU, L_DOWN = 4, 1, 1, 8, 8, 4, 22, 16
L_CHUNKS = L_UG + L_K + L_V + L_QG + L_GC + L_OUT + L_GU + L_DOWN
S_SV, S_U, S_SGU, S_RET, S_AR, S_RO, S_OUT, S_UP, S_DOWN = 4, 4, 8, 12, 4, 4, 4, 22, 16
L_MM = 102
S_CHUNKS = S_SV + S_U + S_SGU + S_RET + S_AR + S_RO + S_OUT + S_UP + S_DOWN
N_CHUNKS = DEPTH * L_CHUNKS + S_CHUNKS

C_ID, C_ONE, C_BD, C_ROT1, C_SEL, C_ROT2, C_MASK = 0, 128, 256, 384, 512, 768, 896
C_N = 1152
A_QN, A_KN, A_SINK, A_CW, A_CB, A_LG, A_LB, A_GF, A_GN = 0, 1, 2, 18, 142, 146, 150, 154, 162
A_N = 170
B_GP, B_GF, B_GO, B_DL, B_G0, B_CV = 0, 8, 16, 24, 32, 40
B_N = B_CV + 8 * FT


class Loops:

    def __init__(self, eng, name, strides):
        self.eng, self.name, self.strides, self.counts, self.n_loops = eng, name, strides, {}, 0

    def park(self, sem):
        self.eng.sem_inc(sem, 1)

    def count(self, sem):
        if sem.name not in self.counts:
            self.counts[sem.name] = Count(self.eng, sem)
        return self.counts[sem.name]

    @contextmanager
    def loop(self, start, end):
        key = (self.name, self.n_loops)
        self.n_loops += 1
        strides = self.strides.setdefault(key, {})
        with self.eng.Fori(start, end) as i:
            outer = {k: (c.base, c.n) for k, c in self.counts.items()}
            for k, c in self.counts.items():
                if strides.get(k, 0):
                    c.base, c.n = self.eng.snap(c.base + c.n + (i - start) * strides[k]), 0
            before = {k: c.n for k, c in self.counts.items()}
            yield i
            for k, c in self.counts.items():
                strides[k] = c.n - before.get(k, 0)
        for k, c in self.counts.items():
            base, n = outer.get(k, (0, 0))
            c.base, c.n = base, n + (end - start) * strides[k]


class Count:

    def __init__(self, eng, sem):
        self.eng, self.sem, self.base, self.n = eng, sem, 0, 0

    def up(self, by=1):
        self.n += by
        return by

    def skip(self, by=1):
        self.n += by

    def next(self, by=1):
        self.n += by
        return self.base + self.n

    def now(self, back=0):
        return self.base + (self.n - back)


def program(nc, W, X, CONST, PARL, PARS, ROPE1, ROPE2, SGT, DIST, OUT, strides):
    with ExitStack() as ctx:
        def sb(name, shape, dt=F32):
            return ctx.enter_context(nc.sbuf_tensor(name, shape, dt))

        raw = sb("w_raw", [P, 2, CH])
        whi = sb("w_hi", [P, 2, CH], F32R)
        wlo = sb("w_lo", [P, 2, CH], F32R)
        x = sb("x", [P, KT, T])
        cst = sb("cst", [P, C_N])
        parl = sb("parl", [P, A_N])
        pars = sb("pars", [P, B_N])
        rstd = sb("rstd", [P, T])
        ssum = sb("ssum", [P, T])
        sq = sb("sq", [P, 2, T])
        tA = sb("tA", [P, T + 2])
        tB = sb("tB", [P, T + 2])
        tC = sb("tC", [P, T])
        tD = sb("tD", [P, T])
        mx = sb("row_max", [P, 8])
        ng = sb("neg_max", [P, 8])
        ls = sb("row_sum", [P, 8])
        es = sb("sink_exp", [P, 8])
        rl = sb("row_scale", [P, 8])
        rt = sb("rstd_col", [P, TB])
        st = sb("bn", [P, 2, 6])
        mv = sb("mean_var", [P, 2])
        sm = sb("small", [P, 6, 8])
        lg = sb("log_gamma", [P, 8])

        def phase(*tensors):
            made = []
            with ExitStack() as inner:
                for name, shape, dt in tensors:
                    made.append(inner.enter_context(nc.sbuf_tensor(name, shape, dt)))
            return made

        z2, _ = phase(("z2", [P, KT, T], F32), ("z2_pad", [P, KT, T], F32))
        xh = sb("in_hi", [P, KT, T], F32R)
        xl = sb("in_lo", [P, KT, T], F32R)
        acth, actl = phase(("act_hi", [P, FT, T], F32R), ("act_lo", [P, FT, T], F32R))
        (ga, y, apad, qh, ql, kh, kl, vh, vl, pr, pth, ptl, rope1, ems) = phase(
            ("gate_a", [P, KT, T], F32), ("conv_y", [P, CT, T], F32), ("conv_in", [P, CT, PADW], F32),
            ("q_hi", [P, 2, T], F32R), ("q_lo", [P, 2, T], F32R), ("k_hi", [P, 2, T], F32R),
            ("k_lo", [P, 2, T], F32R), ("v_hi", [P, TB, 2, 192], F32R), ("v_lo", [P, TB, 2, 192], F32R),
            ("probs", [P, 2, 4, 256], F32), ("pt_hi", [P, 2, 896], F32R), ("pt_lo", [P, 2, 896], F32R),
            ("rope1", [P, 2, T], F32), ("ems", [P, T], F32))
        _, _, cvh, cvl, mh, ml = phase(
            ("gate_a_", [P, KT, T], F32), ("conv_y_", [P, CT, T], F32),
            ("conv_hi", [P, CT, T], F32R), ("conv_lo", [P, CT, T], F32R),
            ("merged_hi", [P, KT, T], F32R), ("merged_lo", [P, KT, T], F32R))
        (us, svh, svl, sv, gtab, btab, _, bsp, wspr, wsph, wspl) = phase(
            ("u_gelu", [P, KT, T], F32), ("sv_hi", [P, TB, D], F32R), ("sv_lo", [P, TB, D], F32R),
            ("sv", [P, TB, D], F32), ("sgu_g", [P, D], F32), ("sgu_b", [P, D], F32), ("sgu_pad", [P, 2 * D], F32),
            ("sgu_bias", [P, SGU_G, P], F32), ("w_sp", [P, SGU_G, P], F32),
            ("w_sp_hi", [P, SGU_G, P], F32R), ("w_sp_lo", [P, SGU_G, P], F32R))
        _, _, _, yh, yl = phase(
            ("u_gelu_", [P, KT, T], F32), ("sv_hi_", [P, TB, D], F32), ("sv_lo_", [P, TB, D], F32),
            ("y_hi", [P, KT, T], F32R), ("y_lo", [P, KT, T], F32R))
        (msgu, og, dtab, rope2, rqh, rql, rkh, rkl, rvh, rvl, rph, rpl) = phase(
            ("msgu", [P, KT, T], F32), ("og", [P, KT, T], F32), ("decay", [P, RH, DWIN], F32),
            ("rope2", [P, 2, T], F32), ("rq_hi", [P, T], F32R), ("rq_lo", [P, T], F32R),
            ("rk_hi", [P, T], F32R), ("rk_lo", [P, T], F32R), ("rv_hi", [P, TB, DV], F32R),
            ("rv_lo", [P, TB, DV], F32R), ("rp_hi", [P, TB, T], F32R), ("rp_lo", [P, TB, T], F32R))
        _, _, dist = phase(("msgu_d", [P, KT, T], F32), ("og_d", [P, KT // 2, T], F32), ("dist", [P, 2, DWIN], F32))
        _, _, ogh, ogl, ar = phase(
            ("msgu_", [P, KT, T], F32), ("og_", [P, KT, T], F32), ("og_hi", [P, KT, T], F32R),
            ("og_lo", [P, KT, T], F32R), ("sig_ar", [P, KT, T], F32))
        z, = phase(("z", [P, KT, T], F32))

        def psum(name, shape):
            return ctx.enter_context(nc.psum_tensor(name, shape, F32))

        mm = [psum("mm0", [P, T]), psum("mm1", [P, T])]
        sp = [psum("sp0", [P, 4, 256]), psum("sp1", [P, 4, 256])]
        spf = [t[:, :, :].rearrange("p a b -> p (a b)") for t in sp]
        ob = psum("ob", [P, T])
        mi = psum("misc", [P, T])

        def sem(name):
            return ctx.enter_context(nc.semaphore(name))

        s_cst = sem("constants_loaded")
        s_par = sem("params_loaded")
        s_tab = sem("tables_loaded")
        s_tab2 = sem("tables2_loaded")
        s_raw = [sem("raw_loaded0"), sem("raw_loaded1")]
        s_whi = sem("w_hi_ready")
        s_w = sem("w_ready")
        s_mm = sem("tile_ready")
        s_half = sem("half_done")
        s_mmf = sem("tile_taken")
        s_ms = sem("misc_ready")
        s_msf = sem("misc_taken")
        s_fn = sem("scalar_value")
        s_val = sem("vector_value")
        s_in = sem("in_ready")
        s_sub = sem("operand_ready")
        s_rot = sem("vector_to_pe")
        s_sqq = sem("head_squares")
        s_sq = sem("square_ready")
        s_sum = sem("square_added")
        s_zs = sem("sum_zeroed")
        s_zero = sem("padding_zeroed")
        s_q = sem("q_ready")
        s_kv = sem("kv_ready")
        s_s = sem("scores_ready")
        s_m = sem("max_ready")
        s_e = sem("exp_ready")
        s_rl = sem("row_scale_ready")
        s_p = sem("probs_ready")
        s_pt = sem("pt_ready")
        s_pth = sem("pt_hi_ready")
        s_ptl = sem("pt_lo_ready")
        s_o = sem("o_ready")
        s_of = sem("o_taken")
        s_ga = sem("gate_ready")
        s_ao = sem("scalar_own")
        s_do = sem("vector_own")
        s_gel = sem("gelu_ready")
        s_fin = sem("x_final")
        s_idle = sem("idle")
        s_out = sem("stored")

        ident = cst[:, C_ID:C_ID + P]
        ones = cst[:, C_ONE:C_ONE + P]
        bd = cst[:, C_BD:C_BD + P]
        rot1 = cst[:, C_ROT1:C_ROT1 + P]
        rot2 = cst[:, C_ROT2:C_ROT2 + P]
        mask = cst[:, C_MASK:C_MASK + 256]
        LEAD = TAPS - 1

        def tile(t, m, lo=0, hi=T):
            if isinstance(m, int):
                return t[:, m, lo:hi]
            return t[:, bass.ds(m, 1), lo:hi].rearrange("p a t -> p (a t)")

        def col(t, c):
            return t[:, c:c + 1] if isinstance(c, int) else t[:, bass.ds(c, 1)]

        def r32(ap):
            return ap.bitcast(F32)

        block = ctx.enter_context(nc.Block())

        @block.sync
        def _(e):
            L = Loops(e, "sp", strides)
            w_free = L.count(s_w)

            def load(n, slot, cols=CH):
                e.wait_ge(s_w, w_free.next())
                e.dma_start(raw[:, slot, 0:cols],
                            W[bass.ds(n, 1), :, 0:cols].rearrange("a p c -> (a p) c")).then_inc(s_raw[slot], 16)

            def stage(n0, pairs, cols=(CH, CH)):
                with L.loop(0, pairs) as i:
                    for c in range(2):
                        load(n0 + i * 2 + c, c, cols[c])

            e.dma_start(x[:, 0:1, :], X[:, 0:1, :]).then_inc(s_cst, 16)
            e.dma_start(pars[:], PARS[:]).then_inc(s_cst, 16)
            e.dma_start(x[:, 1:KT, :], X[:, 1:KT, :]).then_inc(s_cst, 16)
            e.dma_start(cst[:], CONST[:]).then_inc(s_cst, 16)
            with L.loop(0, DEPTH) as l:
                n = e.snap(l * L_CHUNKS)
                load(n, 0)
                load(n + 1, 1)
                e.wait_ge(s_in, l * (2 * KT) + KT)
                e.dma_start(parl[:], PARL[bass.ds(l, 1)].rearrange("a p c -> (a p) c")).then_inc(s_par, 16)
                e.dma_start(rope1[:], ROPE1[:]).then_inc(s_par, 16)
                load(n + 2, 0)
                load(n + 3, 1)
                load(n + L_UG, 0, CH // 2)
                load(n + L_UG + 1, 1, CH // 2)
                n6 = L_UG + L_K + L_V
                stage(n + n6, L_QG // 2)
                stage(n + (n6 + L_QG), L_GC // 2, (CH, CH // 2))
                stage(n + (n6 + L_QG + L_GC), (L_OUT + L_GU) // 2)
                stage(n + (L_CHUNKS - L_DOWN), L_DOWN // 2, (HALF, HALF))
            n = DEPTH * L_CHUNKS
            load(n, 0)
            load(n + 1, 1)
            e.wait_ge(s_mmf, DEPTH * L_MM + 2)
            sg = SGT[:, 2 * D:].rearrange("p (a g q) -> p a g q", a=2, g=SGU_G)
            for t, src in ((gtab, SGT[:, 0:D]), (btab, SGT[:, D:2 * D]), (bsp, sg[:, 0]), (wspr, sg[:, 1])):
                e.dma_start(t[:], src).then_inc(s_tab, 16)
            stage(n + 2, (S_SV + S_U + S_SGU) // 2 - 1)
            n += S_SV + S_U + S_SGU
            load(n, 0)
            load(n + 1, 1)
            e.wait_ge(s_mmf, DEPTH * L_MM + 16 + 8 + 8 + 16 + 2)
            e.dma_start(rope2[:], ROPE2[:]).then_inc(s_tab2, 16)
            e.dma_start(dist[:], DIST[:]).then_inc(s_tab2, 16)
            stage(n + 2, (S_RET + S_AR + S_RO + S_OUT + S_UP) // 2 - 1)
            stage(n + S_RET + S_AR + S_RO + S_OUT + S_UP, S_DOWN // 2, (HALF, HALF))
            for m in range(KT):
                e.wait_ge(s_fin, m + 1)
                e.dma_start(OUT[:, m, :], x[:, m, :]).then_inc(s_out, 16)
            e.wait_ge(s_out, 16 * KT)

        @block.gpsimd
        def _(e):
            L = Loops(e, "pool", strides)
            sq_in, added, zeroed = L.count(s_sq), L.count(s_sum), L.count(s_zs)
            zero, row, probs = L.count(s_zero), L.count(s_rl), L.count(s_p)
            e.sem_inc(s_sum, 2)
            added.skip(2)

            def add_squares():
                e.wait_ge(s_zs, zeroed.next())
                for k in range(KT):
                    e.wait_ge(s_sq, sq_in.next())
                    if k:
                        e.wait_ge(s_sum, added.now())
                    e.tensor_tensor(ssum[:], ssum[:], sq[:, k % 2, :], ALU.add).then_inc(s_sum, added.up())

            add_squares()
            with L.loop(0, DEPTH) as l:
                e.wait_ge(s_mmf, l * L_MM + 2)
                L.park(s_idle)
                e.memset(apad[:, :, 0:LEAD], 0.0).then_inc(s_zero, zero.up())
                for v in (vh, vl):
                    e.memset(r32(v[:, :, :, 0:64]), 0.0).then_inc(s_zero, zero.up())
                    e.memset(r32(v[:, :, :, 128:192]), 0.0).then_inc(s_zero, zero.up())
                for _ in range(QT):
                    for h in range(2):
                        e.wait_ge(s_rl, row.next())
                        L.park(s_idle)
                        for n in range(TB):
                            p = pr[:, h, n, (P if n == 0 else 0):256]
                            last = e.tensor_scalar(p, p, rl[:, 4 * h + n:4 * h + n + 1], None, ALU.mult)
                        last.then_inc(s_p, probs.up())
                add_squares()
                add_squares()
            add_squares()
            add_squares()
            add_squares()

        @block.scalar
        def _(e):
            L = Loops(e, "act", strides)
            whi_out, tiles, half, taken = L.count(s_whi), L.count(s_mm), L.count(s_half), L.count(s_mmf)
            raws = [L.count(s_raw[0]), L.count(s_raw[1])]
            misc_taken, fn, val, own = L.count(s_msf), L.count(s_fn), L.count(s_val), L.count(s_ao)
            sqq, sq_out, added = L.count(s_sqq), L.count(s_sq), L.count(s_sum)
            scores, mxs, ex, pt, pthi, gate = (L.count(s) for s in (s_s, s_m, s_e, s_pt, s_pth, s_ga))
            ofree, gel, par = L.count(s_of), L.count(s_gel), L.count(s_par)
            tiles.skip(1)
            taken.skip(2)
            misc_taken.skip(1)

            def prep(slot, cols=CH, after_half=False):
                e.wait_ge(s_raw[slot], raws[slot].next(16))
                if after_half:
                    e.wait_ge(s_half, half.next())
                else:
                    e.wait_ge(s_mm, tiles.now())
                e.activation(whi[:, slot, 0:cols], raw[:, slot, 0:cols], ACT.Copy).then_inc(s_whi, whi_out.up())

            def inverse_root(src, dst, scale=1.0, signal=None):
                e.activation(src, src, ACT.Ln, scale=scale).then_inc(s_ao, own.up())
                e.wait_ge(s_ao, own.now())
                told = signal or fn
                e.activation(dst, src, ACT.Exp, scale=-0.5).then_inc(told.sem, told.up())

            def hi(dst, src, scale=1.0):
                e.activation(dst, src, ACT.Copy, scale=scale).then_inc(s_fn, fn.up())

            def square(src, k):
                e.activation(tile(sq, k), src, ACT.Square).then_inc(s_sq, sq_out.up())

            e.wait_ge(s_cst, 64)
            e.wait_ge(s_mm, tiles.now())
            e.wait_ge(s_raw[0], raws[0].next(16))
            e.activation(whi[:, 0, :], raw[:, 0, :], ACT.Copy).then_inc(s_whi, whi_out.up())
            for k in range(KT):
                e.wait_ge(s_sum, added.next())
                hi(xh[:, k, :], x[:, k, :], pars[:, B_G0 + k:B_G0 + k + 1])
                square(x[:, k, :], k % 2)

            with L.loop(0, DEPTH) as l:
                e.wait_ge(s_msf, misc_taken.next())
                e.activation(rstd[:], ems[:], ACT.Ln).then_inc(s_ao, own.up())
                e.wait_ge(s_ao, own.now())
                e.activation(rstd[:], rstd[:], ACT.Exp, scale=-0.5).then_inc(s_fn, fn.up())
                with L.loop(0, L_UG // 2) as i:
                    for c in range(2):
                        prep(1 - c)
                        tiles.skip(2)
                        e.wait_ge(s_mmf, taken.next(2))
                        e.activation(tC[:], tB[:, 0:T], ACT.Sigmoid).then_inc(s_fn, fn.up())
                prep(1, CH // 2)
                tiles.skip(1)
                e.wait_ge(s_mmf, taken.next())
                e.activation(sq[:, 1, :], pr[:, 0, 0:2, :].rearrange("p a b -> p (a b)"), ACT.Square).then_inc(s_sqq, sqq.up())
                prep(0)
                tiles.skip(1)
                taken.skip(1)
                e.wait_ge(s_par, par.next(32))
                e.wait_ge(s_msf, misc_taken.next())
                inverse_root(tB[:, 0:T], tC[:], 1.0 / HD)
                for c in range(QT + 2):
                    if c < QT:
                        prep(1 - c % 2)
                        e.wait_ge(s_mm, tiles.next())
                        if c == 0:
                            misc_taken.skip(1)
                        e.activation(sq[:, 0, :], mm[0][:], ACT.Square).then_inc(s_sqq, sqq.up())
                    if 1 <= c <= QT:
                        for h in range(2):
                            e.wait_ge(s_m, mxs.next())
                            head = 2 * (c - 1) + h
                            hs = slice(4 * h, 4 * h + 4)
                            e.activation(es[:, hs], ng[:, hs], ACT.Exp, bias=parl[:, A_SINK + head:A_SINK + head + 1])
                            for n in range(TB):
                                p = pr[:, h, n, (P if n == 0 else 0):256]
                                j = 4 * h + n
                                last = e.activation(p, p, ACT.Exp, bias=ng[:, j:j + 1], accum_out=ls[:, j:j + 1])
                            last.then_inc(s_e, ex.up())
                    if c < QT:
                        e.wait_ge(s_msf, misc_taken.next())
                        inverse_root(tB[:, 0:T], tC[:])
                        if c == 0:
                            e.wait_ge(s_s, scores.next())
                            hi(kh[:, :, :].rearrange("p a t -> p (a t)"), spf[0])
                            e.wait_ge(s_s, scores.next())
                            hi(vh[:, :, :, 64:128], spf[1][:, 0:T].rearrange("p (b k d) -> p b k d", b=TB, k=2))
                        taken.skip(1)
                        misc_taken.skip(1)
                        e.wait_ge(s_val, val.next())
                        hi(qh[:, c % 2, :], tD[:])
                    if 1 <= c <= QT:
                        for h in range(2):
                            e.wait_ge(s_pt, pt.next())
                            e.activation(pth[:, h, :], spf[h][:, 0:896], ACT.Copy).then_inc(s_pth, pthi.up())
                    if c < QT:
                        tiles.skip(1)
                        e.wait_ge(s_mmf, taken.next())
                        e.activation(ga[:, c, :], ga[:, c, :], ACT.Sigmoid).then_inc(s_ga, gate.up())
                scores.skip(2 * QT)
                for t, dst in enumerate((tA[:, 0:T], tC[:], tD[:], sq[:, 0, :])):
                    e.wait_ge(s_val, val.next())
                    e.activation(dst, y[:, t, :], ACT.Square).then_inc(s_fn, fn.up())
                misc_taken.skip(1)
                e.wait_ge(s_msf, misc_taken.next())
                inverse_root(tB[:, 0:T], tC[:])
                for t in range(CT):
                    e.wait_ge(s_val, val.next())
                    e.activation(y[:, t, :], y[:, t, :], ACT.Silu, scale=parl[:, A_LG + t:A_LG + t + 1],
                                            bias=parl[:, A_LB + t:A_LB + t + 1]).then_inc(s_ao, own.up())
                    e.wait_ge(s_ao, own.now())
                    hi(cvh[:, t, :], y[:, t, :])
                with L.loop(0, L_GC // 2) as i:
                    prep(1, CH // 2)
                    tiles.skip(2)
                    e.wait_ge(s_mmf, taken.next(2))
                    e.activation(tA[:, 0:T], tA[:, 0:T], ACT.Sigmoid).then_inc(s_fn, fn.up())
                    e.activation(tB[:, 0:T], tB[:, 0:T], ACT.Sigmoid).then_inc(s_fn, fn.up())
                    prep(0)
                    tiles.skip(2)
                    taken.skip(2)
                    for d in range(2):
                        e.wait_ge(s_val, val.next())
                        hi(tile(mh, i * 2 + d), tD[:])
                with L.loop(0, L_OUT // 2) as i:
                    for c in range(2):
                        prep(1 - c)
                        for d in range(2):
                            m = i * 4 + (2 * c + d)
                            tiles.skip(1)
                            e.wait_ge(s_sum, added.next())
                            e.wait_ge(s_mmf, taken.next())
                            hi(tile(xh, m), tile(x, m), col(parl, m + A_GF))
                            square(tile(x, m), d)
                e.wait_ge(s_msf, misc_taken.next())
                inverse_root(tD[:], rstd[:])
                with L.loop(0, L_GU // 2) as i:
                    for c in range(2):
                        prep(1 - c)
                        tiles.skip(2)
                        e.wait_ge(s_mmf, taken.next())
                        e.activation(tC[:], tA[:, 0:T], ACT.Silu).then_inc(s_fn, fn.up())
                        taken.skip(1)
                        e.wait_ge(s_val, val.next())
                        hi(tile(acth, i * 2 + c), tD[:])
                with L.loop(0, KT // 2) as i:
                    for d in range(2):
                        m = i * 2 + d
                        prep(1, HALF)
                        prep(0, CH, after_half=True)
                        tiles.skip(1)
                        e.wait_ge(s_sum, added.next())
                        e.wait_ge(s_mmf, taken.next())
                        hi(tile(xh, m), tile(x, m), col(parl, m + A_GN))
                        square(tile(x, m), d)

            e.wait_ge(s_val, val.next())
            e.activation(sm[:, 1, :], sm[:, 0, :], ACT.Exp, scale=-1.0).then_inc(s_fn, fn.up())
            e.wait_ge(s_msf, misc_taken.next())
            inverse_root(tD[:], rstd[:], signal=own)
            ofree.skip(QT * DEPTH)
            e.wait_ge(s_of, ofree.next())
            inverse_root(rt[:], rt[:])
            e.wait_ge(s_tab, 64)
            with L.loop(0, S_SV // 2) as i:
                for c in range(2):
                    prep(1 - c)
                    for b in range(TB):
                        tiles.skip(1)
                        e.wait_ge(s_mmf, taken.next())
                        s = sv[:, b, bass.ds(i * 512 + c * 256, 256)]
                        e.activation(s, s, ACT.Gelu_apprx_tanh).then_inc(s_gel, gel.up())
            hi(wsph[:], wspr[:])
            for c in range(S_U):
                prep(1 - c % 2)
                e.wait_ge(s_val, val.next())
                inverse_root(mv[:, 1:2], mv[:, 1:2])
                e.wait_ge(s_val, val.next())
                hi(svh[:, c, :], sv[:, c, :])
                for d in range(2):
                    tiles.skip(1)
                    e.wait_ge(s_mmf, taken.next())
                    e.activation(us[:, 2 * c + d, :], us[:, 2 * c + d, :], ACT.Gelu_apprx_tanh).then_inc(s_fn, fn.up())
            for ct in range(KT):
                tiles.skip(1)
                taken.skip(1)
                e.wait_ge(s_val, val.next())
                hi(yh[:, ct, :], tD[:])
            with L.loop(0, S_SGU // 2) as i:
                prep(1)
                tiles.skip(2)
                e.wait_ge(s_mmf, taken.next(2))
                e.activation(tA[:, 0:T], tA[:, 0:T], ACT.Sigmoid).then_inc(s_fn, fn.up())
                e.activation(tB[:, 0:T], tB[:, 0:T], ACT.Sigmoid).then_inc(s_fn, fn.up())
                prep(0)
                tiles.skip(2)
                taken.skip(2)
            for h in range(RH):
                e.wait_ge(s_val, val.next())
                e.activation(dtab[:, h, :], dtab[:, h, :], ACT.Exp).then_inc(s_fn, fn.up())

            def head():
                def v_hi(b):
                    tiles.skip(1)
                    e.wait_ge(s_mmf, taken.next())
                    hi(rvh[:, b, :], sq[:, b // 2, DV * (b % 2):DV * (b % 2) + DV])

                v_hi(0)
                v_hi(1)
                misc_taken.skip(1)
                e.wait_ge(s_val, val.next())
                hi(rqh[:], tC[:])
                v_hi(2)
                misc_taken.skip(1)
                e.wait_ge(s_val, val.next())
                hi(rkh[:], tC[:])
                v_hi(3)

            def head_rest():
                for mb in range(TB):
                    e.wait_ge(s_val, val.next())
                    hi(rph[:, mb, :], (tC, tD)[mb % 2][:])
                tiles.skip(2)
                e.wait_ge(s_mmf, taken.next(2))
                e.activation(tA[:, 0:T], tA[:, 0:T], ACT.Silu).then_inc(s_fn, fn.up())
                e.activation(tB[:, 0:T], tB[:, 0:T], ACT.Silu).then_inc(s_fn, fn.up())
                misc_taken.skip(1)
                for d in range(2):
                    e.wait_ge(s_val, val.next())
                    e.activation(sq[:, d, :], (tC, tD)[d][:], ACT.Square).then_inc(s_fn, fn.up())
                e.wait_ge(s_msf, misc_taken.next())
                inverse_root(sq[:, 0, :], sq[:, 1, :])

            with L.loop(0, RH // 2) as i:
                for h in range(2):
                    prep(1 - h)
                    tiles.skip(2)
                    taken.skip(2)
                    prep(h)
                    head()
                    prep(1 - h)
                    head_rest()
            with L.loop(0, S_AR // 2) as i:
                for c in range(2):
                    prep(1 - c)
                    for d in range(2):
                        m = i * 4 + (2 * c + d)
                        e.wait_ge(s_val, val.next())
                        hi(tile(ogh, m), tile(og, m))
                        tiles.skip(1)
                        e.wait_ge(s_mmf, taken.next())
                        e.activation(tile(ar, m), tile(ar, m), ACT.Sigmoid).then_inc(s_fn, fn.up())
            with L.loop(0, S_RO // 2) as i:
                for c in range(2):
                    prep(1 - c)
                    for d in range(2):
                        tiles.skip(1)
                        taken.skip(1)
                        e.wait_ge(s_val, val.next())
                        hi(tile(xh, i * 4 + (2 * c + d)), tD[:])
            with L.loop(0, S_OUT // 2) as i:
                for c in range(2):
                    prep(1 - c)
                    for d in range(2):
                        tiles.skip(1)
                        e.wait_ge(s_sum, added.next())
                        e.wait_ge(s_mmf, taken.next())
                        square(tile(z, i * 4 + (2 * c + d)), d)
            e.wait_ge(s_msf, misc_taken.next())
            inverse_root(tD[:], rstd[:])
            for m in range(KT):
                e.wait_ge(s_sum, added.next())
                e.wait_ge(s_val, val.next())
                hi(xh[:, m, :], x[:, m, :], pars[:, B_GF + m:B_GF + m + 1])
                square(x[:, m, :], m % 2)
            e.wait_ge(s_msf, misc_taken.next())
            inverse_root(tD[:], rstd[:])
            with L.loop(0, S_UP // 2) as i:
                for c in range(2):
                    prep(1 - c)
                    b0 = e.snap(i * 16 + (8 * c + B_CV))
                    for hf, src, dst in ((0, tA, tC), (4, tB, tD)):
                        tiles.skip(1)
                        e.wait_ge(s_mmf, taken.next())
                        e.activation(dst[:], src[:, 0:T], ACT.Identity, scale=col(pars, b0 + hf),
                                               bias=col(pars, b0 + (hf + 3))).then_inc(s_fn, fn.up())
                    e.wait_ge(s_val, val.next())
                    e.activation(tC[:], tC[:], ACT.Gelu_apprx_tanh).then_inc(s_fn, fn.up())
                    e.wait_ge(s_val, val.next())
                    hi(tile(acth, i * 2 + c), tD[:])
            with L.loop(0, KT // 2 - 1) as i:
                for d in range(2):
                    prep(1, HALF)
                    prep(0, HALF, after_half=True)
                    tiles.skip(1)
                    e.wait_ge(s_sum, added.next())
                    e.wait_ge(s_mmf, taken.next())
                    square(tile(z2, i * 2 + d), d)
            for m in (KT - 2, KT - 1):
                prep(1, HALF)
                if m < KT - 1:
                    prep(0, HALF, after_half=True)
                tiles.skip(1)
                e.wait_ge(s_sum, added.next())
                e.wait_ge(s_mmf, taken.next())
                square(z2[:, m, :], m % 2)
            e.wait_ge(s_msf, misc_taken.next())
            inverse_root(tD[:], rstd[:])

        @block.vector
        def _(e):
            L = Loops(e, "dve", strides)
            whi_in, w_out, tiles, taken = L.count(s_whi), L.count(s_w), L.count(s_mm), L.count(s_mmf)
            misc, misc_taken, fn, val = L.count(s_ms), L.count(s_msf), L.count(s_fn), L.count(s_val)
            in_out, sub, rot, own = L.count(s_in), L.count(s_sub), L.count(s_rot), L.count(s_do)
            zs, zero, qo, kvo, scores = (L.count(s) for s in (s_zs, s_zero, s_q, s_kv, s_s))
            mxs, ex, row, pthi, ptlo = (L.count(s) for s in (s_m, s_e, s_rl, s_pth, s_ptl))
            o_in, o_taken, gate, gel, par = (L.count(s) for s in (s_o, s_of, s_ga, s_gel, s_par))
            fin = L.count(s_fin)
            e.sem_inc(s_w, 2)
            e.sem_inc(s_mmf, 2)
            e.sem_inc(s_msf, 1)
            e.sem_inc(s_do, 1)
            w_out.skip(2)
            taken.skip(2)
            own.skip(1)
            misc_taken.skip(1)
            tiles.skip(1)
            TT, TS, STT = e.tensor_tensor, e.tensor_scalar, e.scalar_tensor_tensor

            def step(ins):
                ins.then_inc(s_do, own.up())
                e.wait_ge(s_do, own.now())

            def prep(slot, cols=CH):
                e.wait_ge(s_whi, whi_in.next())
                TT(wlo[:, slot, 0:cols], raw[:, slot, 0:cols], r32(whi[:, slot, 0:cols]), ALU.subtract).then_inc(s_w, w_out.up())

            def take(dst, bank, op_in=None):
                e.wait_ge(s_mm, tiles.next())
                TT(dst, mm[bank][:], rstd[:] if op_in is None else op_in, ALU.mult).then_inc(s_mmf, taken.up())

            def mean_square(n, dst):
                e.wait_ge(s_ms, misc.next())
                TS(dst, mi[:], 1.0 / n, EPS, ALU.mult, ALU.add).then_inc(s_msf, misc_taken.up())

            def input_norm(dst):
                mean_square(D, dst)
                e.memset(ssum[:], 0.0).then_inc(s_zs, zs.up())
                e.wait_ge(s_fn, fn.next())

            def lo(dst, src, hi_, out=None):
                e.wait_ge(s_fn, fn.next())
                told = out or sub
                TT(dst, src, r32(hi_), ALU.subtract).then_inc(told.sem, told.up())

            def in_lo(m, g):
                e.wait_ge(s_fn, fn.next())
                STT(tile(xl, m), tile(x, m), g, r32(tile(xh, m)), ALU.mult, ALU.subtract).then_inc(s_in, in_out.up())

            e.memset(ssum[:], 0.0).then_inc(s_zs, zs.up())
            e.wait_ge(s_cst, 64)
            prep(0)
            for k in range(KT):
                in_lo(k, pars[:, B_G0 + k:B_G0 + k + 1])

            taps = [(t, j) for t in range(CT) for j in range(TAPS)]

            def convolve(count):
                for _ in range(min(count, len(taps) - at[0])):
                    t, j = taps[at[0]]
                    at[0] += 1
                    w = parl[:, A_CW + t * TAPS + j:A_CW + t * TAPS + j + 1]
                    a = apad[:, t, j:j + T]
                    if j == 0:
                        TS(y[:, t, :], a, w, parl[:, A_CB + t:A_CB + t + 1], ALU.mult, ALU.add).then_inc(s_do, own.up())
                    else:
                        e.wait_ge(s_do, own.now())
                        STT(y[:, t, :], a, w, y[:, t, :], ALU.mult, ALU.add).then_inc(s_do, own.up())

            with L.loop(0, DEPTH) as l:
                input_norm(ems[:])
                e.wait_ge(s_zero, zero.next(5))
                L.park(s_idle)
                with L.loop(0, L_UG // 2) as i:
                    for c in range(2):
                        prep(1 - c)
                        e.wait_ge(s_do, own.now())
                        take(tA[:, 0:T], 0)
                        take(tB[:, 0:T], 1)
                        e.wait_ge(s_fn, fn.next())
                        e.wait_ge(s_mmf, taken.now())
                        TT(tile(apad, i * 2 + c, LEAD, PADW), tA[:, 0:T], tC[:], ALU.mult).then_inc(s_do, own.up())
                kraw = pr[:, 0, 0:2, :].rearrange("p a b -> p (a b)")
                krot = pr[:, 0, 2:4, :].rearrange("p a b -> p (a b)")
                vval = pr[:, 1, 0:2, :].rearrange("p a b -> p (a b)")
                e.wait_ge(s_par, par.next(32))
                prep(1, CH // 2)
                e.wait_ge(s_mm, tiles.next())
                e.tensor_copy(kraw, mm[0][:]).then_inc(s_mmf, taken.up())
                prep(0)
                take(vval, 1)
                e.wait_ge(s_ms, misc.next())
                STT(tB[:, 0:T], ems[:], HD * EPS, mi[:], ALU.mult, ALU.add).then_inc(s_msf, misc_taken.up())
                e.wait_ge(s_fn, fn.next())
                STT(kraw, kraw, parl[:, A_KN:A_KN + 1], tC[:], ALU.mult, ALU.mult).then_inc(s_rot, rot.up())
                e.wait_ge(s_rot, rot.now())
                TT(krot, kraw, rope1[:, 0, :], ALU.mult).then_inc(s_do, own.up())
                at = [0]
                e.wait_ge(s_do, own.now())
                for c in range(QT + 2):
                    if c < QT:
                        prep(1 - c % 2)
                        convolve(8)
                    if c == 0:
                        e.wait_ge(s_ms, misc.next())
                        TT(tC[:], mi[:], rope1[:, 1, :], ALU.mult).then_inc(s_msf, misc_taken.up())
                        e.wait_ge(s_msf, misc_taken.now())
                        TT(krot, krot, tC[:], ALU.add).then_inc(s_rot, rot.up())
                    if c >= 2:
                        e.wait_ge(s_o, o_in.next())
                        e.wait_ge(s_ga, gate.next())
                        TT(ga[:, c - 2, :], ob[:], ga[:, c - 2, :], ALU.mult).then_inc(s_of, o_taken.up())
                    if 1 <= c <= QT:
                        for h in range(2):
                            e.wait_ge(s_s, scores.next())
                            L.park(s_idle)
                            head = 2 * (c - 1) + h
                            for n in range(TB):
                                w0 = P if n == 0 else 0
                                j = 4 * h + n
                                e.tensor_tensor_reduce(
                                    out=pr[:, h, n, w0:256], in0=sp[h][:, n, w0:256], in1=mask[:, w0:256],
                                    scale=1.0, scalar=parl[:, A_SINK + head:A_SINK + head + 1],
                                    op0=ALU.add, op1=ALU.max, accum_out=mx[:, j:j + 1]).then_inc(s_do, own.up())
                            e.wait_ge(s_do, own.now())
                            TS(ng[:, 4 * h:4 * h + 4], mx[:, 4 * h:4 * h + 4], -1.0, None, ALU.mult).then_inc(s_m, mxs.up())
                    if c < QT:
                        e.wait_ge(s_ms, misc.next())
                        STT(tB[:, 0:T], ems[:], HD * EPS, mi[:], ALU.mult, ALU.add).then_inc(s_msf, misc_taken.up())
                    if 1 <= c <= QT:
                        for h in range(2):
                            e.wait_ge(s_e, ex.next())
                            hs = slice(4 * h, 4 * h + 4)
                            step(TT(ls[:, hs], ls[:, hs], es[:, hs], ALU.add))
                            e.reciprocal(rl[:, hs], ls[:, hs]).then_inc(s_rl, row.up())
                    if c < QT:
                        e.wait_ge(s_fn, fn.next())
                        tiles.skip(1)
                        STT(tD[:], mm[0][:], parl[:, A_QN:A_QN + 1], tC[:], ALU.mult, ALU.mult).then_inc(s_mmf, taken.up())
                        if c == 0:
                            scores.skip(2)
                            lo(kl[:, :, :].rearrange("p a t -> p (a t)"), spf[0], kh[:, :, :].rearrange("p a t -> p (a t)"), kvo)
                            lo(vl[:, :, :, 64:128], spf[1][:, 0:T].rearrange("p (b k d) -> p b k d", b=TB, k=2),
                               vh[:, :, :, 64:128], kvo)
                        e.wait_ge(s_mmf, taken.now())
                        TT(tB[:, 0:T], tD[:], rope1[:, 0, :], ALU.mult).then_inc(s_do, own.up())
                        take(ga[:, c, :], 1)
                        e.wait_ge(s_ms, misc.next())
                        TT(tC[:], mi[:], rope1[:, 1, :], ALU.mult).then_inc(s_msf, misc_taken.up())
                        e.wait_ge(s_msf, misc_taken.now())
                        TT(tD[:], tB[:, 0:T], tC[:], ALU.add).then_inc(s_val, val.up())
                        convolve(8)
                        lo(ql[:, c % 2, :], tD[:], qh[:, c % 2, :], qo)
                    if 1 <= c <= QT:
                        for h in range(2):
                            e.wait_ge(s_pth, pthi.next())
                            TT(ptl[:, h, :], spf[h][:, 0:896], r32(pth[:, h, :]), ALU.subtract).then_inc(s_ptl, ptlo.up())
                e.wait_ge(s_do, own.now())
                step(TT(tA[:, 0:T], y[:, 0, :], y[:, 1, :], ALU.add))
                step(TT(tA[:, 0:T], tA[:, 0:T], y[:, 2, :], ALU.add))
                TT(tA[:, 0:T], tA[:, 0:T], y[:, 3, :], ALU.add).then_inc(s_rot, rot.up())
                e.wait_ge(s_ms, misc.next())
                TS(tB[:, 0:T], mi[:], 1.0 / CONV_CH, None, ALU.mult).then_inc(s_msf, misc_taken.up())
                e.wait_ge(s_msf, misc_taken.now())
                for t in range(CT):
                    TT(y[:, t, :], y[:, t, :], tB[:, 0:T], ALU.subtract).then_inc(s_val, val.up())
                e.wait_ge(s_fn, fn.next(4))
                step(TT(tA[:, 0:T], tA[:, 0:T], tC[:], ALU.add))
                step(TT(tA[:, 0:T], tA[:, 0:T], tD[:], ALU.add))
                TT(tA[:, 0:T], tA[:, 0:T], sq[:, 0, :], ALU.add).then_inc(s_rot, rot.up())
                mean_square(CONV_CH, tB[:, 0:T])
                e.wait_ge(s_fn, fn.next())
                for t in range(CT):
                    TT(y[:, t, :], y[:, t, :], tC[:], ALU.mult).then_inc(s_val, val.up())
                for t in range(CT):
                    lo(cvl[:, t, :], y[:, t, :], cvh[:, t, :])
                with L.loop(0, L_GC // 2) as i:
                    prep(1, CH // 2)
                    take(tA[:, 0:T], 0)
                    take(tB[:, 0:T], 1)
                    prep(0)
                    e.wait_ge(s_fn, fn.next(2))
                    for d in range(2):
                        take(tC[:], d, (tA, tB)[d][:, 0:T])
                        e.wait_ge(s_mmf, taken.now())
                        m = i * 2 + d
                        TT(tD[:], tC[:], tile(ga, m), ALU.add).then_inc(s_val, val.up())
                        lo(tile(ml, m), tD[:], tile(mh, m))
                with L.loop(0, L_OUT // 2) as i:
                    for c in range(2):
                        prep(1 - c)
                        for d in range(2):
                            m = i * 4 + (2 * c + d)
                            e.wait_ge(s_mm, tiles.next())
                            TT(tile(x, m), mm[d][:], tile(x, m), ALU.add).then_inc(s_mmf, taken.up())
                            in_lo(m, col(parl, m + A_GF))
                input_norm(tD[:])
                L.park(s_idle)
                with L.loop(0, L_GU // 2) as i:
                    for c in range(2):
                        prep(1 - c)
                        take(tA[:, 0:T], 0)
                        take(tB[:, 0:T], 1)
                        e.wait_ge(s_fn, fn.next())
                        e.wait_ge(s_mmf, taken.now())
                        TT(tD[:], tC[:], tB[:, 0:T], ALU.mult).then_inc(s_val, val.up())
                        lo(tile(actl, i * 2 + c), tD[:], tile(acth, i * 2 + c))
                with L.loop(0, KT // 2) as i:
                    for d in range(2):
                        m = i * 2 + d
                        prep(1, HALF)
                        prep(0)
                        e.wait_ge(s_mm, tiles.next())
                        TT(tile(x, m), mm[d][:], tile(x, m), ALU.add).then_inc(s_mmf, taken.up())
                        in_lo(m, col(parl, m + A_GN))

            v, zz, s1, s2, pz, tmp = (sm[:, j, :] for j in range(6))
            logit = pars[:, B_DL:B_DL + 8]
            step(TS(tmp, logit, -1.0, None, ALU.mult))
            TT(v, logit, tmp, ALU.max).then_inc(s_val, val.up())
            e.wait_ge(s_fn, fn.next())
            step(TS(s2, zz, 2.0, None, ALU.add))
            step(e.reciprocal(s1, s2))
            step(TT(s1, s1, zz, ALU.mult))
            step(TT(s2, s1, s1, ALU.mult))
            step(TS(pz, s2, 1.0 / 17, 1.0 / 15, ALU.mult, ALU.add))
            for odd in (13, 11, 9, 7, 5, 3, 1):
                step(TT(pz, pz, s2, ALU.mult))
                step(TS(pz, pz, 1.0 / odd, None, ALU.add))
            step(TT(pz, pz, s1, ALU.mult))
            step(TS(tmp, logit, 0.0, None, ALU.min))
            STT(lg[:], pz, -2.0, tmp, ALU.mult, ALU.add).then_inc(s_do, own.up())

            mean_square(D, tD[:])
            e.wait_ge(s_o, o_in.next())
            TS(rt[:], ob[:, 0:TB], 1.0 / D, EPS, ALU.mult, ALU.add).then_inc(s_of, o_taken.up())
            e.memset(ssum[:], 0.0).then_inc(s_zs, zs.up())
            e.wait_ge(s_fn, fn.next())
            with L.loop(0, S_SV // 2) as i:
                for c in range(2):
                    prep(1 - c)
                    for b in range(TB):
                        e.wait_ge(s_mm, tiles.next())
                        TS(sv[:, b, bass.ds(i * 512 + c * 256, 256)], mm[b % 2][:, 0:256],
                                        rt[:, b:b + 1], None, ALU.mult).then_inc(s_mmf, taken.up())
            e.wait_ge(s_tab, 64)
            lo(wspl[:], wspr[:], wsph[:])
            e.wait_ge(s_gel, gel.next(4 * S_SV))
            for c in range(S_U):
                prep(1 - c % 2)
                e.bn_stats(st[:, 0, :], sv[:, c, 0:512]).then_inc(s_do, own.up())
                step(e.bn_stats(st[:, 1, :], sv[:, c, 512:1024]))
                step(e.bn_aggr(mv[:], st[:, :, :].rearrange("p a b -> p (a b)")))
                TS(mv[:, 1:2], mv[:, 1:2], EPS, None, ALU.add).then_inc(s_val, val.up())
                e.wait_ge(s_fn, fn.next(3 if c else 1))
                step(TS(sv[:, c, :], sv[:, c, :], mv[:, 0:1], mv[:, 1:2], ALU.subtract, ALU.mult))
                step(TT(sv[:, c, :], sv[:, c, :], gtab[:], ALU.mult))
                TT(sv[:, c, :], sv[:, c, :], btab[:], ALU.add).then_inc(s_val, val.up())
                lo(svl[:, c, :], sv[:, c, :], svh[:, c, :])
                for d in range(2):
                    take(us[:, 2 * c + d, :], d)
            e.wait_ge(s_fn, fn.next(2))
            for ct in range(KT):
                e.wait_ge(s_mm, tiles.next())
                bias = bsp[:, ct // 2, :].rearrange("p (a q) -> p a q", a=1).broadcast_to([P, TB, P])
                TT(tA[:, 0:T].rearrange("p (a q) -> p a q", a=TB),
                                mm[ct % 2][:].rearrange("p (a q) -> p a q", a=TB), bias, ALU.add).then_inc(s_mmf, taken.up())
                e.wait_ge(s_mmf, taken.now())
                TT(tD[:], tA[:, 0:T], us[:, ct, :], ALU.mult).then_inc(s_val, val.up())
                lo(yl[:, ct, :], tD[:], yh[:, ct, :])
            with L.loop(0, S_SGU // 2) as i:
                prep(1)
                take(tA[:, 0:T], 0)
                take(tB[:, 0:T], 1)
                prep(0)
                e.wait_ge(s_fn, fn.next(2))
                for d in range(2):
                    take(tile(msgu, i * 2 + d), d, (tA, tB)[d][:, 0:T])
            e.wait_ge(s_tab2, 32)
            for h in range(RH):
                step(TS(dtab[:, h, :], dist[:, 0, :], lg[:, h:h + 1], None, ALU.mult))
                STT(dtab[:, h, :], dist[:, 1, :], lg[:, RH + h:RH + h + 1], dtab[:, h, :], ALU.mult, ALU.add).then_inc(s_val, val.up())
            e.wait_ge(s_fn, fn.next(RH))

            def v_take(b):
                e.wait_ge(s_mm, tiles.next())
                vt = sq[:, b // 2, DV * (b % 2):DV * (b % 2) + DV]
                TS(vt, mm[b % 2][:, 0:DV], rt[:, b:b + 1], None, ALU.mult).then_inc(s_mmf, taken.up())
                lo(rvl[:, b, :], vt, rvh[:, b, :])

            def rotate(src, scale, dst_hi, dst_lo):
                STT(tC[:], src[:, 0:T], scale, rope2[:, 0, :], ALU.mult, ALU.mult).then_inc(s_do, own.up())
                e.wait_ge(s_ms, misc.next())
                STT(tD[:], mi[:], scale, rope2[:, 1, :], ALU.mult, ALU.mult).then_inc(s_msf, misc_taken.up())
                e.wait_ge(s_msf, misc_taken.now())
                TT(tC[:], tC[:], tD[:], ALU.add).then_inc(s_val, val.up())
                lo(dst_lo[:], tC[:], dst_hi[:], qo)

            with L.loop(0, RH // 2) as i:
                for h in range(2):
                    hd = i * 2 + h
                    prep(1 - h)
                    e.wait_ge(s_do, own.now())
                    take(tA[:, 0:T], 0)
                    take(tB[:, 0:T], 1)
                    prep(h)
                    v_take(0)
                    v_take(1)
                    rotate(tA, 1.0, rqh, rql)
                    v_take(2)
                    rotate(tB, float(DK) ** -0.5, rkh, rkl)
                    v_take(3)
                    prep(1 - h)
                    for mb in range(TB):
                        e.wait_ge(s_s, scores.next())
                        t = (tC, tD)[mb % 2]
                        win = (TB - 1 - mb) * P
                        TT(t[:], spf[mb // 2][:, T * (mb % 2):T * (mb % 2) + T],
                                      tile(dtab, hd, win, win + T), ALU.mult).then_inc(s_val, val.up())
                        lo(rpl[:, mb, :], t[:], rph[:, mb, :])
                    take(tA[:, 0:T], 0)
                    take(tB[:, 0:T], 1)
                    e.wait_ge(s_fn, fn.next(2))
                    e.wait_ge(s_o, o_in.next())
                    e.tensor_copy(tC[:], ob[:]).then_inc(s_do, own.up())
                    e.wait_ge(s_o, o_in.next())
                    step(e.tensor_copy(tD[:], spf[0][:, 0:T]))
                    TT(sq[:, 0, :], tC[:], tD[:], ALU.add).then_inc(s_rot, rot.up())
                    e.wait_ge(s_ms, misc.next())
                    TS(sq[:, 1, :], mi[:], 1.0 / DV, None, ALU.mult).then_inc(s_msf, misc_taken.up())
                    e.wait_ge(s_msf, misc_taken.now())
                    TT(tC[:], tC[:], sq[:, 1, :], ALU.subtract).then_inc(s_val, val.up())
                    TT(tD[:], tD[:], sq[:, 1, :], ALU.subtract).then_inc(s_val, val.up())
                    e.wait_ge(s_fn, fn.next(2))
                    TT(sq[:, 0, :], sq[:, 0, :], sq[:, 1, :], ALU.add).then_inc(s_rot, rot.up())
                    mean_square(DV, sq[:, 0, :])
                    e.wait_ge(s_fn, fn.next())
                    for d, t, g in ((0, tC, tA), (1, tD, tB)):
                        step(TT(t[:], t[:], sq[:, 1, :], ALU.mult))
                        TT(tile(og, i * 4 + (2 * h + d)), t[:], g[:, 0:T], ALU.mult).then_inc(s_do, own.up())
            with L.loop(0, S_AR // 2) as i:
                for c in range(2):
                    prep(1 - c)
                    for d in range(2):
                        m = i * 4 + (2 * c + d)
                        e.wait_ge(s_do, own.now())
                        e.memset(sm[:, 5, 0:1], 0.0).then_inc(s_val, val.up())
                        lo(tile(ogl, m), tile(og, m), tile(ogh, m))
                        take(tile(ar, m), d)
                        e.wait_ge(s_fn, fn.next())
            with L.loop(0, S_RO // 2) as i:
                for c in range(2):
                    prep(1 - c)
                    for d in range(2):
                        m = i * 4 + (2 * c + d)
                        take(tA[:, 0:T], d, tile(ar, m))
                        e.wait_ge(s_mmf, taken.now())
                        TT(tD[:], tA[:, 0:T], tile(msgu, m), ALU.add).then_inc(s_val, val.up())
                        lo(tile(xl, m), tD[:], tile(xh, m), in_out)
            with L.loop(0, S_OUT // 2) as i:
                for c in range(2):
                    prep(1 - c)
                    for d in range(2):
                        e.wait_ge(s_mm, tiles.next())
                        e.tensor_copy(tile(z, i * 4 + (2 * c + d)), mm[d][:]).then_inc(s_mmf, taken.up())
            e.wait_ge(s_mmf, taken.now())
            input_norm(tD[:])
            for m in range(KT):
                step(STT(tA[:, 0:T], z[:, m, :], pars[:, B_GP + m:B_GP + m + 1], rstd[:], ALU.mult, ALU.mult))
                TT(x[:, m, :], x[:, m, :], tA[:, 0:T], ALU.add).then_inc(s_val, val.up())
                in_lo(m, pars[:, B_GF + m:B_GF + m + 1])
            for t in (tA, tB):
                e.memset(t[:, 0:1], 0.0).then_inc(s_do, own.up())
                e.memset(t[:, T + 1:T + 2], 0.0).then_inc(s_do, own.up())
            input_norm(tD[:])
            with L.loop(0, S_UP // 2) as i:
                for c in range(2):
                    prep(1 - c)
                    b0 = e.snap(i * 16 + (8 * c + B_CV))
                    take(tA[:, 1:T + 1], 0)
                    take(tB[:, 1:T + 1], 1)
                    for hf, src, dst in ((0, tA, tC), (4, tB, tD)):
                        e.wait_ge(s_fn, fn.next())
                        e.wait_ge(s_mmf, taken.now())
                        step(STT(dst[:], src[:, 1:T + 1], col(pars, b0 + (hf + 1)), dst[:], ALU.mult, ALU.add))
                        told = own if hf else val
                        STT(dst[:], src[:, 2:T + 2], col(pars, b0 + (hf + 2)), dst[:], ALU.mult, ALU.add).then_inc(told.sem, told.up())
                    e.wait_ge(s_do, own.now())
                    e.wait_ge(s_fn, fn.next())
                    TT(tD[:], tC[:], tD[:], ALU.mult).then_inc(s_val, val.up())
                    lo(tile(actl, i * 2 + c), tD[:], tile(acth, i * 2 + c))
            with L.loop(0, KT // 2 - 1) as i:
                for d in range(2):
                    prep(1, HALF)
                    prep(0, HALF)
                    e.wait_ge(s_mm, tiles.next())
                    e.tensor_copy(tile(z2, i * 2 + d), mm[d][:]).then_inc(s_mmf, taken.up())
            for m in (KT - 2, KT - 1):
                prep(1, HALF)
                if m < KT - 1:
                    prep(0, HALF)
                e.wait_ge(s_mm, tiles.next())
                e.tensor_copy(z2[:, m, :], mm[m % 2][:]).then_inc(s_mmf, taken.up())
            mean_square(D, tD[:])
            e.wait_ge(s_mmf, taken.now())
            e.wait_ge(s_fn, fn.next())
            for m in range(KT):
                if m:
                    e.wait_ge(s_fin, fin.now())
                step(STT(tA[:, 0:T], z2[:, m, :], pars[:, B_GO + m:B_GO + m + 1], rstd[:], ALU.mult, ALU.mult))
                TT(x[:, m, :], x[:, m, :], tA[:, 0:T], ALU.add).then_inc(s_fin, fin.up())

        @block.tensor
        def _(e):
            L = Loops(e, "pe", strides)
            w_in, tiles, half, taken = L.count(s_w), L.count(s_mm), L.count(s_half), L.count(s_mmf)
            misc, misc_taken, inp, sub, rot = (L.count(s) for s in (s_ms, s_msf, s_in, s_sub, s_rot))
            sqq, added, q_in, kv_in, scores = (L.count(s) for s in (s_sqq, s_sum, s_q, s_kv, s_s))
            probs, pt, ptlo, o_out = (L.count(s) for s in (s_p, s_pt, s_ptl, s_o))
            e.sem_inc(s_mm, 1)
            w_in.skip(2)
            tiles.skip(1)
            added.skip(2)
            MM = e.matmul

            def mm3(out, ah, al, bh, bl, first, last, **kw):
                MM(out, ah, bh, start=first, stop=False, **kw)
                MM(out, ah, bl, start=False, stop=False, **kw)
                return MM(out, al, bh, start=False, stop=last, **kw)

            def product(bank, slot, at, hi_, lo_, ks, ready=None, first=True, last=True):
                for j, k in enumerate(ks):
                    if ready is not None:
                        e.wait_ge(ready.sem, ready.next())
                    a = slice((at + j) * P, (at + j + 1) * P)
                    ins = mm3(mm[bank][:], whi[:, slot, a], wlo[:, slot, a], hi_[:, k, :], lo_[:, k, :],
                              first and j == 0, last and j == len(ks) - 1)
                return ins

            def out_tile(bank, slot, at, hi_, lo_, n_k, ready=None):
                e.wait_ge(s_mmf, taken.next())
                product(bank, slot, at, hi_, lo_, range(n_k), ready).then_inc(s_mm, tiles.up())

            def small(lhs, rhs, src=None):
                if src is not None:
                    e.wait_ge(src.sem, src.next())
                e.wait_ge(s_msf, misc_taken.next())
                MM(mi[:], lhs, rhs, start=True, stop=True).then_inc(s_ms, misc.up())

            def token_sums():
                e.wait_ge(s_sum, added.next(KT))
                small(ones, ssum[:])

            def pair(hi_, lo_, ready=None, norm=False):
                for c in range(2):
                    e.wait_ge(s_w, w_in.next())
                    for d in range(2):
                        out_tile(d, c, KT * d, hi_, lo_, KT, ready if c == d == 0 else None)
                        if norm and c == d == 0:
                            token_sums()

            def down():

                def two(ready):
                    for d in range(2):
                        e.wait_ge(s_w, w_in.next())
                        e.wait_ge(s_mmf, taken.next())
                        product(d, 0, 0, acth, actl, range(FT // 2), None if d else ready, last=False).then_inc(s_half, half.up())
                        e.wait_ge(s_w, w_in.next())
                        product(d, 1, 0, acth, actl, range(FT // 2, FT), None if d else ready, first=False).then_inc(s_mm, tiles.up())

                two(sub)
                with L.loop(1, KT // 2):
                    two(None)

            def attend(s, h):
                a = slice(64 * h, 64 * h + 64)
                for n in range(TB):
                    k0 = max(n - 1, 0) * P
                    qs = slice(n * P, (n + 1) * P)
                    ks = slice(k0, (n + 1) * P)
                    ins = mm3(sp[h][:, n, (P if n == 0 else 0):256], qh[a, s % 2, qs], ql[a, s % 2, qs],
                              kh[a, s // 4, ks], kl[a, s // 4, ks], True, True)
                ins.then_inc(s_s, scores.up())

            def turn(h):
                e.wait_ge(s_p, probs.next())
                for j in range(TB):
                    ins = e.transpose(spf[h][:, 256 * j:256 * j + P], pr[:, h, j, P:256], ident)
                    if j + 1 < TB:
                        ins = e.transpose(spf[h][:, 256 * j + P:256 * j + 256], pr[:, h, j + 1, 0:P], ident)
                ins.then_inc(s_pt, pt.up())

            def weigh(s):
                e.wait_ge(s_ptl, ptlo.next(2))
                for h in range(2):
                    for j in range(TB):
                        n = 2 * P if j + 1 < TB else P
                        v = slice(64 - 64 * h, 192 - 64 * h)
                        cs = slice(256 * j, 256 * j + n)
                        ins = mm3(ob[:, j * P:j * P + n], vh[:, j, s // 4, v], vl[:, j, s // 4, v],
                                  pth[:, h, cs], ptl[:, h, cs], h == j == 0, h == 1 and j == TB - 1,
                                  skip_group_check=True)
                ins.then_inc(s_o, o_out.up())

            e.wait_ge(s_cst, 64)
            with L.loop(0, DEPTH) as l:
                pair(xh, xl, inp, norm=True)
                with L.loop(1, L_UG // 2):
                    pair(xh, xl)
                e.wait_ge(s_w, w_in.next())
                out_tile(0, 0, 0, xh, xl, KT)
                e.wait_ge(s_w, w_in.next())
                out_tile(1, 1, 0, xh, xl, KT)
                small(bd, sq[:, 1, :], sqq)
                for c in range(QT + 2):
                    if c < QT:
                        e.wait_ge(s_w, w_in.next())
                        out_tile(0, c % 2, 0, xh, xl, KT)
                        if c == 0:
                            small(rot1, pr[:, 0, 0:2, :].rearrange("p a b -> p (a b)"), rot)
                    if c >= 2:
                        weigh(c - 2)
                    if 1 <= c <= QT:
                        e.wait_ge(s_q, q_in.next())
                        if c == 1:
                            e.wait_ge(s_kv, kv_in.next(2))
                        attend(c - 1, 0)
                        attend(c - 1, 1)
                    if c < QT:
                        small(bd, sq[:, 0, :], sqq)
                        out_tile(1, c % 2, KT, xh, xl, KT)
                        if c == 0:
                            e.wait_ge(s_rot, rot.next())
                            for kv in range(2):
                                sel = cst[:, C_SEL + kv * P:C_SEL + (kv + 1) * P]
                                ins = MM(spf[0][:, kv * T:(kv + 1) * T], sel,
                                         pr[:, 0, 2:4, :].rearrange("p a b -> p (a b)"), start=True, stop=True)
                            ins.then_inc(s_s, scores.up())
                            for b in range(TB):
                                ins = e.transpose(spf[1][:, b * P:(b + 1) * P],
                                                  pr[:, 1, b // 2, (b % 2) * P:(b % 2) * P + P], ident)
                            ins.then_inc(s_s, scores.up())
                        e.wait_ge(s_mmf, taken.now(-1))
                        small(rot1, tD[:])
                    if 1 <= c <= QT:
                        turn(0)
                        turn(1)
                e.wait_ge(s_w, w_in.next())
                out_tile(0, 0, 0, xh, xl, KT)
                small(ones, tA[:, 0:T], rot)
                out_tile(1, 0, KT, xh, xl, KT)
                small(ones, tA[:, 0:T], rot)
                e.wait_ge(s_w, w_in.next())
                e.wait_ge(s_sub, sub.next(CT))
                out_tile(0, 1, 0, cvh, cvl, CT)
                out_tile(1, 1, CT, cvh, cvl, CT)
                with L.loop(1, L_GC // 2):
                    e.wait_ge(s_w, w_in.next())
                    out_tile(0, 0, 0, xh, xl, KT)
                    out_tile(1, 0, KT, xh, xl, KT)
                    e.wait_ge(s_w, w_in.next())
                    out_tile(0, 1, 0, cvh, cvl, CT)
                    out_tile(1, 1, CT, cvh, cvl, CT)
                pair(mh, ml, sub)
                with L.loop(1, L_OUT // 2):
                    pair(mh, ml)
                pair(xh, xl, inp, norm=True)
                with L.loop(1, L_GU // 2):
                    pair(xh, xl)
                down()

            def token_major(slot, bank, b, ready=None):
                e.wait_ge(s_mmf, taken.next())
                ts = slice(b * P, (b + 1) * P)
                for k in range(KT):
                    if ready is not None:
                        e.wait_ge(ready.sem, ready.next())
                    ws = slice(256 * k, 256 * k + 256)
                    ins = mm3(mm[bank][:, 0:256], xh[:, k, ts], xl[:, k, ts], whi[:, slot, ws], wlo[:, slot, ws],
                              k == 0, k == KT - 1)
                ins.then_inc(s_mm, tiles.up())

            e.wait_ge(s_w, w_in.next())
            token_major(0, 0, 0, inp)
            token_sums()
            for b in range(TB):
                ins = MM(ob[:, b:b + 1], ssum[:, b * P:(b + 1) * P], ones[:, 0:1], start=True, stop=True)
            ins.then_inc(s_o, o_out.up())
            for b in range(1, TB):
                token_major(0, b % 2, b)
            e.wait_ge(s_w, w_in.next())
            for b in range(TB):
                token_major(1, b % 2, b)
            with L.loop(1, S_SV // 2):
                for c in range(2):
                    e.wait_ge(s_w, w_in.next())
                    for b in range(TB):
                        token_major(c, b % 2, b)
            with L.loop(0, S_U // 2):
                pair(xh, xl)
            e.wait_ge(s_sub, sub.next(1 + TB))
            for ct in range(KT):
                e.wait_ge(s_mmf, taken.next())
                for n in range(TB):
                    ins = mm3(mm[ct % 2][:, n * P:(n + 1) * P], svh[:, n, ct * P:(ct + 1) * P],
                              svl[:, n, ct * P:(ct + 1) * P], wsph[:, ct // 2, :], wspl[:, ct // 2, :], True, True)
                ins.then_inc(s_mm, tiles.up())

            def gate_and_out(ready):
                e.wait_ge(s_w, w_in.next())
                out_tile(0, 0, 0, xh, xl, KT)
                out_tile(1, 0, KT, xh, xl, KT)
                e.wait_ge(s_w, w_in.next())
                out_tile(0, 1, 0, yh, yl, KT, ready)
                out_tile(1, 1, KT, yh, yl, KT)

            gate_and_out(sub)
            with L.loop(1, S_SGU // 2):
                gate_and_out(None)

            def retain(h):
                e.wait_ge(s_w, w_in.next())
                out_tile(0, h, 0, xh, xl, KT)
                out_tile(1, h, KT, xh, xl, KT)
                e.wait_ge(s_w, w_in.next())
                token_major(1 - h, 0, 0)
                token_major(1 - h, 1, 1)
                small(rot2, tA[:, 0:T])
                token_major(1 - h, 0, 2)
                small(rot2, tB[:, 0:T])
                token_major(1 - h, 1, 3)
                e.wait_ge(s_q, q_in.next(2))
                for mb in range(TB):
                    cs = slice(mb * P, (mb + 1) * P)
                    mm3(spf[mb // 2][:, T * (mb % 2):T * (mb % 2) + T], rkh[:, cs], rkl[:, cs],
                                      rqh[:], rql[:], True, True).then_inc(s_s, scores.up())
                e.wait_ge(s_w, w_in.next())
                out_tile(0, h, 0, xh, xl, KT)
                out_tile(1, h, KT, xh, xl, KT)
                e.wait_ge(s_sub, sub.next(2 * TB))
                for d, dst in ((0, ob[:]), (1, spf[0][:, 0:T])):
                    for mb in range(TB):
                        cs = slice(d * P, (d + 1) * P)
                        ins = mm3(dst, rvh[:, mb, cs], rvl[:, mb, cs], rph[:, mb, :], rpl[:, mb, :],
                                  mb == 0, mb == TB - 1)
                    ins.then_inc(s_o, o_out.up())
                small(ones, sq[:, 0, :], rot)
                small(ones, sq[:, 0, :], rot)

            with L.loop(0, RH // 2):
                retain(0)
                retain(1)
            with L.loop(0, S_AR // 2):
                pair(xh, xl)
            pair(ogh, ogl, sub)
            with L.loop(1, S_RO // 2):
                pair(ogh, ogl)
            pair(xh, xl, inp)
            with L.loop(1, S_OUT // 2):
                pair(xh, xl)
            token_sums()
            pair(xh, xl, inp, norm=True)
            with L.loop(1, S_UP // 2):
                pair(xh, xl)
            down()
            token_sums()



def constants():
    c = np.zeros((P, C_N), np.float32)
    c[:, C_ID:C_ID + P] = np.eye(P)
    c[:, C_ONE:C_ONE + P] = 1.0
    i = np.arange(P)
    c[:, C_BD:C_BD + P] = i[:, None] // HD == i[None, :] // HD
    half = ROT // 2
    for h in range(2):
        for d in range(half):
            c[h * HD + d + half, C_ROT1 + h * HD + d] = -1.0
            c[h * HD + d, C_ROT1 + h * HD + d + half] = 1.0
    for kv in range(2):
        for d in range(P):
            c[kv * HD + d % HD, C_SEL + kv * P + d] = 1.0
    for d in range(DK // 2):
        c[d + DK // 2, C_ROT2 + d] = -1.0
        c[d, C_ROT2 + d + DK // 2] = 1.0
    j = np.arange(256)
    rel = i[:, None] + P - j[None, :]
    c[:, C_MASK:C_MASK + 256] = np.where((rel >= 0) & (rel < P), 0.0, -1e30)
    return c


def rope_tables(theta, rot, width):
    half = rot // 2
    inv = (np.float32(theta) ** (-np.arange(0, rot, 2, dtype=np.float32) / np.float32(rot))).astype(np.float32)
    ang = (np.arange(T, dtype=np.float32)[:, None] * inv[None, :]).astype(np.float32)
    t = np.zeros((P, 2, T), np.float32)
    t[:, 0] = 1.0
    for base in range(0, P, width):
        for d in range(half):
            for r in (base + d, base + d + half):
                t[r, 0] = np.cos(ang[:, d])
                t[r, 1] = np.sin(ang[:, d])
    return t


def distances():
    d = np.arange(DWIN)[None, :] - (TB - 1) * P - np.arange(P)[:, None]
    return np.stack([np.maximum(d, 0), np.maximum(-d, 0)], 1).astype(np.float32)


def kernel(**inputs):
    import concourse.bacc as bacc
    from concourse.bass_utils import run_bass_kernel_spmd as run

    a = {k: np.asarray(v) for k, v in inputs.items()}
    W = np.zeros((N_CHUNKS, P, CH), np.float32)
    at = [0]

    def tiles_chunk(*tiles):
        c = 0
        for m, c0 in tiles:
            kt = m.shape[0] // P
            W[at[0], :, c:c + kt * P] = m[:, c0:c0 + P].reshape(kt, P, P).transpose(1, 0, 2).reshape(P, kt * P)
            c += kt * P
        at[0] += 1

    def columns_chunk(m, c0):
        W[at[0]] = m[:, c0:c0 + 256].reshape(KT, P, 256).transpose(1, 0, 2).reshape(P, CH)
        at[0] += 1

    def all_tiles(m):
        for c in range(0, KT, 2):
            tiles_chunk((m, c * P), (m, (c + 1) * P))

    def up_chunks(m):
        for t in range(FT):
            tiles_chunk((m, t * P), (m, FF + t * P))

    def down_chunks(m):
        for c in range(KT):
            for h in range(2):
                tiles_chunk((m[h * HALF:(h + 1) * HALF], c * P))

    parl = np.zeros((DEPTH, P, A_N), np.float32)
    pars = np.zeros((P, B_N), np.float32)
    by_tile = lambda v: v.reshape(-1, P).T
    q_w, kv_w = HEADS * HD, KV_HEADS * HD
    u0 = q_w + 2 * kv_w
    ga0 = u0 + 2 * CONV_CH
    for l in range(DEPTH):
        w = a["w_in"][l]
        for t in range(CT):
            tiles_chunk((w, u0 + t * P), (w, u0 + CONV_CH + t * P))
        tiles_chunk((w, q_w))
        tiles_chunk((w, q_w + kv_w))
        for t in range(QT):
            tiles_chunk((w, t * P), (w, ga0 + t * P))
        for t in range(0, KT, 2):
            tiles_chunk((w, ga0 + D + t * P), (w, ga0 + D + (t + 1) * P))
            tiles_chunk((a["w_conv_out"][l], t * P), (a["w_conv_out"][l], (t + 1) * P))
        all_tiles(a["w_out"][l])
        up_chunks(a["w_gate_up"][l])
        down_chunks(a["w_down"][l])
        p = parl[l]
        p[:, A_QN] = np.tile(a["q_norm"][l], 2)
        p[:, A_KN] = np.tile(a["k_norm"][l], 2)
        p[:, A_SINK:A_SINK + HEADS] = np.broadcast_to(a["sinks"][l], (P, HEADS))
        p[:, A_CW:A_CW + CT * TAPS] = a["conv_w"][l].reshape(TAPS, CT, P).transpose(2, 1, 0).reshape(P, CT * TAPS)
        p[:, A_CB:A_CB + CT] = by_tile(a["conv_b"][l])
        p[:, A_LG:A_LG + CT] = by_tile(a["conv_ln_g"][l])
        p[:, A_LB:A_LB + CT] = by_tile(a["conv_ln_b"][l])
        p[:, A_GF:A_GF + KT] = by_tile(a["norm_ffn"][l])
        p[:, A_GN:A_GN + KT] = by_tile(a["norm_mix"][l + 1] if l + 1 < DEPTH else a["g_pre_mix_2"])
    w = a["w_in_2"]
    offs = np.cumsum([0, RH * DK, RH * DK, RH * DV, RH * DV, D, D, D])
    q0, k0, v0, g0, us0, sv0, ar0, as0 = (int(o) for o in offs)
    for c in range(S_SV):
        columns_chunk(w, sv0 + 256 * c)
    for t in range(0, KT, 2):
        tiles_chunk((w, us0 + t * P), (w, us0 + (t + 1) * P))
    for t in range(0, KT, 2):
        tiles_chunk((w, as0 + t * P), (w, as0 + (t + 1) * P))
        tiles_chunk((a["w_sgu_o_2"], t * P), (a["w_sgu_o_2"], (t + 1) * P))
    for h in range(RH):
        tiles_chunk((w, q0 + h * DK), (w, k0 + h * DK))
        columns_chunk(w, v0 + h * DV)
        tiles_chunk((w, g0 + h * DV), (w, g0 + h * DV + P))
    all_tiles(w[:, ar0:ar0 + D])
    all_tiles(a["w_ret_o_2"])
    all_tiles(a["w_out_2"])
    up_chunks(a["w_up_2"])
    down_chunks(a["w_down_2"])
    assert at[0] == N_CHUNKS
    pars[:, B_GP:B_GP + KT] = by_tile(a["g_post_mix_2"])
    pars[:, B_GF:B_GF + KT] = by_tile(a["g_pre_ffn_2"])
    pars[:, B_GO:B_GO + KT] = by_tile(a["g_post_ffn_2"])
    pars[:, B_G0:B_G0 + KT] = by_tile(a["norm_mix"][0])
    pars[:, B_DL:B_DL + 2 * RH] = np.broadcast_to(a["ret_decay_logit_2"].reshape(-1), (P, 2 * RH))
    cv = np.concatenate([a["conv_w_2"], a["conv_b_2"][None]], 0)
    pars[:, B_CV:] = cv.reshape(4, 2, FT, P).transpose(3, 2, 1, 0).reshape(P, 8 * FT)
    sgt = np.zeros((P, 2 * D + 2 * SGU_G * P), np.float32)
    sgt[:, 0:D] = np.broadcast_to(a["sgu_ln_g_2"], (P, D))
    sgt[:, D:2 * D] = np.broadcast_to(a["sgu_ln_b_2"], (P, D))
    sgt[:, 2 * D:2 * D + SGU_G * P] = np.broadcast_to(a["b_spatial_2"].reshape(-1), (P, SGU_G * P))
    sgt[:, 2 * D + SGU_G * P:] = a["w_spatial_2"].transpose(2, 0, 1).reshape(P, SGU_G * P)
    xt = np.ascontiguousarray(a["x"][0].T.reshape(KT, P, T).transpose(1, 0, 2))
    arrays = {"w": W, "x": xt, "const": constants(), "par_l": parl, "par_s": pars,
              "rope1": rope_tables(500000.0, ROT, HD), "rope2": rope_tables(10000.0, DK, DK),
              "sgu_tables": sgt, "distances": distances()}

    strides = {}
    for _ in range(2):
        nc = bacc.Bacc("TRN2", target_bir_lowering=False, num_devices=1)
        args = [nc.dram_tensor(f"in_{n}_dram", v.shape, F32, kind="ExternalInput").ap() for n, v in arrays.items()]
        args.append(nc.dram_tensor("out_0_dram", (P, KT, T), F32, kind="ExternalOutput").ap())
        program(nc, *args, strides)
    r = run(nc, [{f"in_{n}_dram": v for n, v in arrays.items()}], core_ids=[0])
    got = r.results[0]["out_0_dram"]
    return np.ascontiguousarray(got.transpose(2, 1, 0).reshape(1, T, D))
```

```python
from contextlib import ExitStack, contextmanager

import concourse.bass as bass
from concourse import mybir
import numpy as np

ALU = mybir.AluOpType
ACT = mybir.ActivationFunctionType
F32 = mybir.dt.float32
F32R = mybir.dt.float32r
AX_X = mybir.AxisListType.X

P = 128
D = 1024
T = 512
KT = D // P
TB = T // P
DEPTH = 2
HEADS, KV_HEADS, HD = 16, 2, 64
QT = HEADS * HD // P
CONV_CH, TAPS = 512, 31
CT = CONV_CH // P
PADW = T + TAPS - 1
FF = 2816
FT = FF // P
EPS = 1e-6
ROT = HD // 4
RH, DK, DV = 4, 128, 256
SGU_G = 4
DWIN = T + (TB - 1) * P
CH = 2048
HALF = FT // 2 * P
TAPS_U, TAPS_KV = (7, 8, 8, 8), 6
TAPS_ATT = (6, 5) + (QT - 2) * (4,) + (12, 9)
VT = CT - 1
assert sum(TAPS_U) + TAPS_KV + sum(TAPS_ATT) == VT * TAPS
LN_EXP = "natural_log_exp_and_others"

L_UG, L_KV, L_QG, L_GB, L_CO, L_OUT, L_GU, L_DOWN = 4, 2, 8, 4, 2, 4, 22, 16
L_CHUNKS = L_UG + L_KV + L_QG + L_GB + L_CO + L_OUT + L_GU + L_DOWN
S_SV, S_U, S_SGU, S_RET, S_AR, S_RO, S_OUT, S_UP, S_DOWN = 4, 4, 8, 12, 4, 4, 4, 22, 16
L_MM = 102
S_CHUNKS = S_SV + S_U + S_SGU + S_RET + S_AR + S_RO + S_OUT + S_UP + S_DOWN
N_CHUNKS = DEPTH * L_CHUNKS + S_CHUNKS

C_ID, C_ONE, C_BD, C_ROT1, C_SEL, C_ROT2, C_MASK = 0, 128, 256, 384, 512, 768, 896
C_N = 1152
A_QN, A_KN, A_SINK, A_CW, A_CB, A_LG, A_LB, A_GF, A_GN = 0, 1, 2, 18, 142, 146, 150, 154, 162
A_N = 170
B_GP, B_GF, B_GO, B_DL, B_G0, B_CV = 0, 8, 16, 24, 32, 40
B_N = B_CV + 8 * FT


class Loops:

    def __init__(self, eng, name, strides):
        self.eng, self.name, self.strides, self.counts, self.n_loops = eng, name, strides, {}, 0

    def park(self, sem):
        self.eng.sem_inc(sem, 1)

    def count(self, sem):
        if sem.name not in self.counts:
            self.counts[sem.name] = Count(self.eng, sem)
        return self.counts[sem.name]

    @contextmanager
    def loop(self, start, end):
        key = (self.name, self.n_loops)
        self.n_loops += 1
        strides = self.strides.setdefault(key, {})
        with self.eng.Fori(start, end) as i:
            outer = {k: (c.base, c.n) for k, c in self.counts.items()}
            for k, c in self.counts.items():
                if strides.get(k, 0):
                    c.base, c.n = self.eng.snap(c.base + c.n + (i - start) * strides[k]), 0
            before = {k: c.n for k, c in self.counts.items()}
            yield i
            for k, c in self.counts.items():
                strides[k] = c.n - before.get(k, 0)
        for k, c in self.counts.items():
            base, n = outer.get(k, (0, 0))
            c.base, c.n = base, n + (end - start) * strides[k]


class Count:

    def __init__(self, eng, sem):
        self.eng, self.sem, self.base, self.n = eng, sem, 0, 0

    def up(self, by=1):
        self.n += by
        return by

    def skip(self, by=1):
        self.n += by

    def next(self, by=1):
        self.n += by
        return self.base + self.n

    def now(self, back=0):
        return self.base + (self.n - back)


def program(nc, W, X, CONST, PARL, PARS, ROPE1, ROPE2, SGT, DIST, OUT, strides):
    with ExitStack() as ctx:
        def sb(name, shape, dt=F32):
            return ctx.enter_context(nc.sbuf_tensor(name, shape, dt))

        raw = sb("w_raw", [P, 2, CH])
        whi = sb("w_hi", [P, 2, CH], F32R)
        wlo = sb("w_lo", [P, 2, CH], F32R)
        x = sb("x", [P, KT, T])
        cst = sb("cst", [P, C_N])
        parl = sb("parl", [P, A_N])
        pars = sb("pars", [P, B_N])
        rstd = sb("rstd", [P, T])
        ssum = sb("ssum", [P, T])
        sq = sb("sq", [P, 2, T])
        tA = sb("tA", [P, T + 2])
        tB = sb("tB", [P, T + 2])
        tC = sb("tC", [P, T])
        tD = sb("tD", [P, T])
        mx = sb("row_max", [P, 8])
        ng = sb("neg_max", [P, 8])
        ls = sb("row_sum", [P, 8])
        es = sb("sink_exp", [P, 8])
        rl = sb("row_scale", [P, 8])
        rt = sb("rstd_col", [P, TB])
        st = sb("bn", [P, 2, 6])
        mv = sb("mean_var", [P, 2])
        sm = sb("small", [P, 6, 8])
        lg = sb("log_gamma", [P, 8])

        def phase(*tensors):
            made = []
            with ExitStack() as inner:
                for name, shape, dt in tensors:
                    made.append(inner.enter_context(nc.sbuf_tensor(name, shape, dt)))
            return made

        z2, _ = phase(("z2", [P, KT, T], F32), ("z2_pad", [P, KT, T], F32))
        xh = sb("in_hi", [P, KT, T], F32R)
        xl = sb("in_lo", [P, KT, T], F32R)
        acth, actl = phase(("act_hi", [P, FT, T], F32R), ("act_lo", [P, FT, T], F32R))
        (ga, y, apad, qh, ql, kh, kl, vh, vl, pr, pth, ptl, rope1, ems) = phase(
            ("gate_a", [P, KT, T], F32), ("conv_y", [P, CT, T], F32), ("conv_in", [P, CT, PADW], F32),
            ("q_hi", [P, 2, T], F32R), ("q_lo", [P, 2, T], F32R), ("k_hi", [P, 2, T], F32R),
            ("k_lo", [P, 2, T], F32R), ("v_hi", [P, TB, 2, 192], F32R), ("v_lo", [P, TB, 2, 192], F32R),
            ("probs", [P, 2, 4, 256], F32), ("pt_hi", [P, 2, 896], F32R), ("pt_lo", [P, 2, 896], F32R),
            ("rope1", [P, 2, T], F32), ("ems", [P, T], F32))
        _, _, cvh, _, gb2, gb4, gb3, mh, ml, cvl, gb67, gb01, gb5 = phase(
            ("gate_a_", [P, KT, T], F32), ("conv_y_", [P, CT, T], F32), ("conv_hi", [P, CT, T], F32R),
            ("conv_pad", [P, CT, PADW - T], F32), ("gate_b2", [P, T], F32), ("gate_b4", [P, T], F32),
            ("gate_b3", [P, T], F32), ("merged_hi", [P, KT, T], F32R), ("merged_lo", [P, KT, T], F32R),
            ("conv_lo", [P, CT, T], F32R), ("gate_b67", [P, 2, T], F32), ("gate_b01", [P, 2, T], F32),
            ("gate_b5", [P, T], F32))
        gb = [gb01[:, 0, :], gb01[:, 1, :], gb2[:], gb3[:], gb4[:], gb5[:], gb67[:, 0, :], gb67[:, 1, :]]
        (us, svh, svl, sv, gtab, btab, _, bsp, wspr, wsph, wspl) = phase(
            ("u_gelu", [P, KT, T], F32), ("sv_hi", [P, TB, D], F32R), ("sv_lo", [P, TB, D], F32R),
            ("sv", [P, TB, D], F32), ("sgu_g", [P, D], F32), ("sgu_b", [P, D], F32), ("sgu_pad", [P, 2 * D], F32),
            ("sgu_bias", [P, SGU_G, P], F32), ("w_sp", [P, SGU_G, P], F32),
            ("w_sp_hi", [P, SGU_G, P], F32R), ("w_sp_lo", [P, SGU_G, P], F32R))
        _, _, _, yh, yl = phase(
            ("u_gelu_", [P, KT, T], F32), ("sv_hi_", [P, TB, D], F32), ("sv_lo_", [P, TB, D], F32),
            ("y_hi", [P, KT, T], F32R), ("y_lo", [P, KT, T], F32R))
        (msgu, og, dtab, rope2, rqh, rql, rkh, rkl, rvh, rvl, rph, rpl) = phase(
            ("msgu", [P, KT, T], F32), ("og", [P, KT, T], F32), ("decay", [P, RH, DWIN], F32),
            ("rope2", [P, 2, T], F32), ("rq_hi", [P, T], F32R), ("rq_lo", [P, T], F32R),
            ("rk_hi", [P, T], F32R), ("rk_lo", [P, T], F32R), ("rv_hi", [P, TB, DV], F32R),
            ("rv_lo", [P, TB, DV], F32R), ("rp_hi", [P, TB, T], F32R), ("rp_lo", [P, TB, T], F32R))
        _, _, dist = phase(("msgu_d", [P, KT, T], F32), ("og_d", [P, KT // 2, T], F32), ("dist", [P, 2, DWIN], F32))
        _, _, ogh, ogl, ar = phase(
            ("msgu_", [P, KT, T], F32), ("og_", [P, KT, T], F32), ("og_hi", [P, KT, T], F32R),
            ("og_lo", [P, KT, T], F32R), ("sig_ar", [P, KT, T], F32))
        z, = phase(("z", [P, KT, T], F32))

        def psum(name, shape):
            return ctx.enter_context(nc.psum_tensor(name, shape, F32))

        mm = [psum("mm0", [P, T]), psum("mm1", [P, T])]
        sp = [psum("sp0", [P, 4, 256]), psum("sp1", [P, 4, 256])]
        spf = [t[:, :, :].rearrange("p a b -> p (a b)") for t in sp]
        ob = psum("ob", [P, T])
        mi = psum("misc", [P, T])

        def sem(name):
            return ctx.enter_context(nc.semaphore(name))

        s_x0 = sem("first_tile_loaded")
        s_x1 = sem("x_loaded")
        s_cst = sem("constants_loaded")
        s_par = sem("params_loaded")
        s_tab = sem("tables_loaded")
        s_tab2 = sem("tables2_loaded")
        s_raw = [sem("raw_loaded0"), sem("raw_loaded1")]
        s_whi = sem("w_hi_ready")
        s_w = sem("w_ready")
        s_mm = sem("tile_ready")
        s_half = sem("half_done")
        s_mmf = sem("tile_taken")
        s_ms = sem("misc_ready")
        s_msf = sem("misc_taken")
        s_fn = sem("scalar_value")
        s_val = sem("vector_value")
        s_in = sem("in_ready")
        s_sub = sem("operand_ready")
        s_rot = sem("vector_to_pe")
        s_sqq = sem("head_squares")
        s_sq = sem("square_ready")
        s_sum = sem("square_added")
        s_zs = sem("sum_zeroed")
        s_zero = sem("padding_zeroed")
        s_q = sem("q_ready")
        s_kv = sem("kv_ready")
        s_s = sem("scores_ready")
        s_m = sem("max_ready")
        s_e = sem("exp_ready")
        s_p = sem("probs_ready")
        s_r2 = sem("root_squared")
        s_root = sem("root_ready")
        s_po = sem("pool_own")
        s_pt = sem("pt_ready")
        s_pth = sem("pt_hi_ready")
        s_ptl = sem("pt_lo_ready")
        s_o = sem("o_ready")
        s_of = sem("o_taken")
        s_ga = sem("gate_ready")
        s_ao = sem("scalar_own")
        s_do = sem("vector_own")
        s_gel = sem("gelu_ready")
        s_og = sem("retention_ready")
        s_tap = sem("tap_product")
        s_acc = sem("tap_added")
        s_fin = sem("x_final")
        s_idle = sem("idle")
        s_out = sem("stored")

        ident = cst[:, C_ID:C_ID + P]
        ones = cst[:, C_ONE:C_ONE + P]
        bd = cst[:, C_BD:C_BD + P]
        rot1 = cst[:, C_ROT1:C_ROT1 + P]
        rot2 = cst[:, C_ROT2:C_ROT2 + P]
        mask = cst[:, C_MASK:C_MASK + 256]
        LEAD = TAPS - 1

        def tile(t, m, lo=0, hi=T):
            if isinstance(m, int):
                return t[:, m, lo:hi]
            return t[:, bass.ds(m, 1), lo:hi].rearrange("p a t -> p (a t)")

        def col(t, c):
            return t[:, c:c + 1] if isinstance(c, int) else t[:, bass.ds(c, 1)]

        def r32(ap):
            return ap.bitcast(F32)

        block = ctx.enter_context(nc.Block())

        @block.sync
        def _(e):
            L = Loops(e, "sp", strides)
            w_free = L.count(s_w)

            def load(n, slot, cols=CH):
                e.wait_ge(s_w, w_free.next())
                e.dma_start(raw[:, slot, 0:cols],
                            W[bass.ds(n, 1), :, 0:cols].rearrange("a p c -> (a p) c")).then_inc(s_raw[slot], 16)

            def stage(n0, pairs, cols=(CH, CH)):
                with L.loop(0, pairs) as i:
                    for c in range(2):
                        load(n0 + i * 2 + c, c, cols[c])

            e.dma_start(x[:, 0:1, :], X[:, 0:1, :]).then_inc(s_x0, 16)
            e.dma_start(pars[:], PARS[:]).then_inc(s_x0, 16)
            load(0, 0)
            e.dma_start(x[:, 1:KT, :], X[:, 1:KT, :]).then_inc(s_x1, 16)
            load(1, 1)
            e.dma_start(cst[:], CONST[:]).then_inc(s_cst, 16)
            with L.loop(0, DEPTH) as l:
                n = e.snap(l * L_CHUNKS)
                e.wait_ge(s_in, l * (2 * KT) + KT)
                e.dma_start(parl[:], PARL[bass.ds(l, 1)].rearrange("a p c -> (a p) c")).then_inc(s_par, 16)
                e.dma_start(rope1[:], ROPE1[:]).then_inc(s_par, 16)
                load(n + 2, 0)
                load(n + 3, 1)
                load(n + L_UG, 0, CH // 2)
                load(n + L_UG + 1, 1, CH // 2)
                stage(n + (L_UG + L_KV), (L_QG + L_GB + L_CO + L_OUT + L_GU) // 2)
                stage(n + (L_CHUNKS - L_DOWN), L_DOWN // 2, (HALF, HALF))
                load(n + L_CHUNKS, 0)
                load(n + (L_CHUNKS + 1), 1)
            n = DEPTH * L_CHUNKS
            e.wait_ge(s_mmf, DEPTH * L_MM + 2)
            sg = SGT[:, 2 * D:].rearrange("p (a g q) -> p a g q", a=2, g=SGU_G)
            for t, src in ((gtab, SGT[:, 0:D]), (btab, SGT[:, D:2 * D]), (bsp, sg[:, 0]), (wspr, sg[:, 1])):
                e.dma_start(t[:], src).then_inc(s_tab, 16)
            stage(n + 2, (S_SV + S_U + S_SGU) // 2 - 1)
            n += S_SV + S_U + S_SGU
            load(n, 0)
            load(n + 1, 1)
            e.wait_ge(s_mmf, DEPTH * L_MM + 16 + 8 + 8 + 16 + 2)
            e.dma_start(rope2[:], ROPE2[:]).then_inc(s_tab2, 16)
            e.dma_start(dist[:], DIST[:]).then_inc(s_tab2, 16)
            stage(n + 2, (S_RET + S_AR + S_RO + S_OUT + S_UP) // 2 - 1)
            stage(n + S_RET + S_AR + S_RO + S_OUT + S_UP, S_DOWN // 2, (HALF, HALF))
            for m in range(KT):
                e.wait_ge(s_fin, m + 1)
                e.dma_start(OUT[:, m, :], x[:, m, :]).then_inc(s_out, 16)
            e.wait_ge(s_out, 16 * KT)

        @block.gpsimd
        def _(e):
            L = Loops(e, "pool", strides)
            sq_in, added, zeroed = L.count(s_sq), L.count(s_sum), L.count(s_zs)
            zero, r2, root, own = L.count(s_zero), L.count(s_r2), L.count(s_root), L.count(s_po)
            product, summed = L.count(s_tap), L.count(s_acc)
            e.sem_inc(s_sum, 2)
            e.sem_inc(s_acc, 1)
            added.skip(2)
            summed.skip(1)

            def add_squares():
                e.wait_ge(s_zs, zeroed.next())
                for k in range(KT):
                    e.wait_ge(s_sq, sq_in.next())
                    if k:
                        e.wait_ge(s_sum, added.now())
                    e.tensor_tensor(ssum[:], ssum[:], sq[:, k % 2, :], ALU.add).then_inc(s_sum, added.up())

            def newton():
                e.wait_ge(s_r2, r2.next())
                e.tensor_tensor(sq[:, 1, :], sq[:, 1, :], tB[:, 0:T], ALU.mult).then_inc(s_po, own.up())
                e.wait_ge(s_po, own.now())
                L.park(s_idle)
                e.tensor_scalar(sq[:, 1, :], sq[:, 1, :], -0.5, 1.5, ALU.mult, ALU.add).then_inc(s_po, own.up())
                e.wait_ge(s_po, own.now())
                e.tensor_tensor(tC[:], tC[:], sq[:, 1, :], ALU.mult).then_inc(s_root, root.up())

            def add_taps(j0, count):
                for j in range(j0, min(j0 + count, TAPS)):
                    e.wait_ge(s_tap, product.next())
                    if j == 0:
                        e.sem_inc(s_acc, summed.up())
                    else:
                        e.wait_ge(s_acc, summed.now())
                        e.tensor_tensor(y[:, VT, :], y[:, VT, :], ssum[:], ALU.add).then_inc(s_acc, summed.up())

            add_squares()
            with L.loop(0, DEPTH) as l:
                e.wait_ge(s_mmf, l * L_MM + 2)
                L.park(s_idle)
                e.memset(apad[:, :, 0:LEAD], 0.0).then_inc(s_zero, zero.up())
                for v in (vh, vl):
                    e.memset(r32(v[:, :, :, 0:64]), 0.0).then_inc(s_zero, zero.up())
                    e.memset(r32(v[:, :, :, 128:192]), 0.0).then_inc(s_zero, zero.up())
                newton()
                add_taps(0, 3)
                for c in range(QT):
                    add_taps(4 * c + 3, 1)
                    newton()
                    add_taps(4 * c + 4, 3)
                add_squares()
                add_squares()
            add_squares()
            add_squares()
            add_squares()

        @block.scalar
        def _(e):
            L = Loops(e, "act", strides)
            whi_out, tiles, half, taken = L.count(s_whi), L.count(s_mm), L.count(s_half), L.count(s_mmf)
            raws = [L.count(s_raw[0]), L.count(s_raw[1])]
            misc_taken, fn, val, own = L.count(s_msf), L.count(s_fn), L.count(s_val), L.count(s_ao)
            sqq, sq_out, added = L.count(s_sqq), L.count(s_sq), L.count(s_sum)
            scores, mxs, ex, pt, pthi, gate = (L.count(s) for s in (s_s, s_m, s_e, s_pt, s_pth, s_ga))
            ofree, gel, par, r2 = L.count(s_of), L.count(s_gel), L.count(s_par), L.count(s_r2)
            ogs, product, summed = L.count(s_og), L.count(s_tap), L.count(s_acc)
            summed.skip(1)
            tiles.skip(1)
            taken.skip(2)
            misc_taken.skip(1)

            def prep(slot, cols=CH, after_half=False):
                e.wait_ge(s_raw[slot], raws[slot].next(16))
                if after_half:
                    e.wait_ge(s_half, half.next())
                else:
                    e.wait_ge(s_mm, tiles.now())
                e.activation(whi[:, slot, 0:cols], raw[:, slot, 0:cols], ACT.Copy).then_inc(s_whi, whi_out.up())

            def inverse_root(src, dst, signal=None):
                e.activation(src, src, ACT.Ln).then_inc(s_ao, own.up())
                e.wait_ge(s_ao, own.now())
                told = signal or fn
                e.activation(dst, src, ACT.Exp, scale=-0.5).then_inc(told.sem, told.up())

            def hi(dst, src, scale=1.0):
                e.activation(dst, src, ACT.Copy, scale=scale).then_inc(s_fn, fn.up())

            def square(src, k):
                e.activation(tile(sq, k), src, ACT.Square).then_inc(s_sq, sq_out.up())

            def head_root():
                e.wait_ge(s_msf, misc_taken.next())
                e.activation(sq[:, 1, :], tB[:, 0:T], ACT.Ln).then_inc(s_ao, own.up())
                e.wait_ge(s_ao, own.now())
                e.activation(tC[:], sq[:, 1, :], ACT.Exp, scale=-0.5).then_inc(s_ao, own.up())
                e.wait_ge(s_ao, own.now())
                e.activation(sq[:, 1, :], tC[:], ACT.Square).then_inc(s_r2, r2.up())

            def tap_products(j0, count):
                for j in range(j0, min(j0 + count, TAPS)):
                    w = parl[:, A_CW + VT * TAPS + j:A_CW + VT * TAPS + j + 1]
                    a = apad[:, VT, j:j + T]
                    e.wait_ge(s_acc, summed.now())
                    summed.skip(1)
                    if j == 0:
                        e.activation(y[:, VT, :], a, ACT.Identity, scale=w,
                                     bias=parl[:, A_CB + VT:A_CB + VT + 1]).then_inc(s_tap, product.up())
                    else:
                        e.activation(ssum[:], a, ACT.Copy, scale=w).then_inc(s_tap, product.up())

            e.wait_ge(s_x0, 32)
            prep(0)
            for k in range(KT):
                if k == 1:
                    e.wait_ge(s_x1, 16)
                e.wait_ge(s_sum, added.next())
                hi(xh[:, k, :], x[:, k, :], pars[:, B_G0 + k:B_G0 + k + 1])
                square(x[:, k, :], k % 2)
            prep(1)

            with L.loop(0, DEPTH) as l:
                e.preload_act_table_set(LN_EXP)
                e.wait_ge(s_msf, misc_taken.next())
                e.activation(rstd[:], ems[:], ACT.Ln).then_inc(s_ao, own.up())
                e.wait_ge(s_ao, own.now())
                e.activation(rstd[:], rstd[:], ACT.Exp, scale=-0.5).then_inc(s_fn, fn.up())
                for c in range(L_UG):
                    tiles.skip(2)
                    prep(c % 2, CH if c < L_UG - L_KV else CH // 2)
                    e.wait_ge(s_mmf, taken.next(2))
                    e.activation(tC[:], tB[:, 0:T], ACT.Sigmoid).then_inc(s_fn, fn.up())
                tiles.skip(1)
                prep(0)
                e.wait_ge(s_mmf, taken.next())
                e.activation(sq[:, 1, :], pr[:, 0, 0:2, :].rearrange("p a b -> p (a b)"),
                             ACT.Square).then_inc(s_sqq, sqq.up())
                e.preload_act_table_set(LN_EXP)
                e.wait_ge(s_par, par.next(32))
                head_root()
                tiles.skip(1)
                taken.skip(1)
                prep(1)
                tap_products(0, 3)
                for c in range(QT + 2):
                    if c < QT:
                        e.wait_ge(s_mm, tiles.next())
                        if c == 0:
                            misc_taken.skip(1)
                        e.activation(sq[:, 0, :], mm[0][:], ACT.Square).then_inc(s_sqq, sqq.up())
                        tap_products(4 * c + 3, 1)
                    if c >= 2:
                        for h in range(2):
                            e.wait_ge(s_pt, pt.next())
                            e.activation(pth[:, h, :], spf[h][:, 0:896], ACT.Copy).then_inc(s_pth, pthi.up())
                    if c < QT:
                        head_root()
                        if c == 0:
                            e.wait_ge(s_s, scores.next())
                            hi(kh[:, :, :].rearrange("p a t -> p (a t)"), spf[0])
                            e.wait_ge(s_s, scores.next())
                            hi(vh[:, :, :, 64:128], spf[1][:, 0:T].rearrange("p (b k d) -> p b k d", b=TB, k=2))
                        tiles.skip(1)
                        e.wait_ge(s_mmf, taken.next(2))
                        e.activation(ga[:, c, :], ga[:, c, :], ACT.Sigmoid).then_inc(s_ga, gate.up())
                        tap_products(4 * c + 4, 1)
                    else:
                        tiles.skip(2)
                        for d in range(2):
                            g = gb[2 * (c - QT) + d]
                            e.wait_ge(s_mmf, taken.next())
                            e.activation(g, g, ACT.Sigmoid).then_inc(s_ga, gate.up())
                    if c <= QT:
                        e.preload_act_table_set(LN_EXP)
                    if 1 <= c <= QT:
                        for h in range(2):
                            e.wait_ge(s_m, mxs.next())
                            head = 2 * (c - 1) + h
                            hs = slice(4 * h, 4 * h + 4)
                            e.activation(es[:, hs], ng[:, hs], ACT.Exp, bias=parl[:, A_SINK + head:A_SINK + head + 1])
                            for n in range(TB):
                                p = pr[:, h, n, (P if n == 0 else 0):256]
                                j = 4 * h + n
                                last = e.activation(p, p, ACT.Exp, bias=ng[:, j:j + 1], accum_out=ls[:, j:j + 1])
                            last.then_inc(s_e, ex.up())
                    if c < QT:
                        misc_taken.skip(1)
                        e.wait_ge(s_val, val.next())
                        hi(qh[:, c % 2, :], tD[:])
                        tap_products(4 * c + 5, 1)
                    prep(c % 2)
                    if c < QT:
                        tap_products(4 * c + 6, 1)
                scores.skip(2 * QT)
                for t, dst in enumerate((tA[:, 0:T], tC[:], tD[:], sq[:, 0, :])):
                    e.wait_ge(s_val, val.next())
                    e.activation(dst, y[:, t, :], ACT.Square).then_inc(s_fn, fn.up())
                tiles.skip(2)
                prep(0)
                misc_taken.skip(1)
                e.preload_act_table_set(LN_EXP)
                e.wait_ge(s_msf, misc_taken.next())
                inverse_root(tB[:, 0:T], tC[:])
                for t in range(CT):
                    e.wait_ge(s_val, val.next())
                    e.activation(y[:, t, :], y[:, t, :], ACT.Silu, scale=parl[:, A_LG + t:A_LG + t + 1],
                                 bias=parl[:, A_LB + t:A_LB + t + 1]).then_inc(s_ao, own.up())
                    e.wait_ge(s_ao, own.now())
                    hi(cvh[:, t, :], y[:, t, :])
                tiles.skip(2)
                prep(1)
                for g in gb[4:]:
                    e.wait_ge(s_mmf, taken.next())
                    e.activation(g, g, ACT.Sigmoid).then_inc(s_ga, gate.up())
                for m in range(KT):
                    tiles.skip(1)
                    taken.skip(1)
                    if m % 4 == 3:
                        prep(m // 4)
                    e.wait_ge(s_val, val.next())
                    hi(mh[:, m, :], (tD, tB)[m % 2][:, 0:T])
                with L.loop(0, L_OUT // 2) as i:
                    for c in range(2):
                        for d in range(2):
                            m = i * 4 + (2 * c + d)
                            tiles.skip(1)
                            if d:
                                prep(c)
                            e.wait_ge(s_sum, added.next())
                            e.wait_ge(s_mmf, taken.next())
                            hi(tile(xh, m), tile(x, m), col(parl, m + A_GF))
                            square(tile(x, m), d)
                e.preload_act_table_set(LN_EXP)
                e.wait_ge(s_msf, misc_taken.next())
                inverse_root(tD[:], rstd[:])

                def gated(m, c, cols=CH):
                    tiles.skip(2)
                    prep(c, cols)
                    e.wait_ge(s_mmf, taken.next())
                    e.activation(tC[:], tA[:, 0:T], ACT.Silu).then_inc(s_fn, fn.up())
                    taken.skip(1)
                    e.wait_ge(s_val, val.next())
                    hi(tile(acth, m), tD[:])

                with L.loop(0, L_GU // 2 - 1) as i:
                    gated(i * 2, 0)
                    gated(i * 2 + 1, 1)
                gated(FT - 2, 0, HALF)
                gated(FT - 1, 1, HALF)

                def down(m, d, cols=HALF):
                    prep(0, cols, after_half=True)
                    tiles.skip(1)
                    prep(1, cols)
                    e.wait_ge(s_sum, added.next())
                    e.wait_ge(s_mmf, taken.next())
                    hi(tile(xh, m), tile(x, m), col(parl, m + A_GN))
                    square(tile(x, m), d)

                with L.loop(0, KT // 2 - 1) as i:
                    down(i * 2, 0)
                    down(i * 2 + 1, 1)
                down(KT - 2, 0)
                down(KT - 1, 1, CH)

            e.wait_ge(s_val, val.next())
            e.activation(sm[:, 1, :], sm[:, 0, :], ACT.Exp, scale=-1.0).then_inc(s_fn, fn.up())
            e.preload_act_table_set(LN_EXP)
            e.wait_ge(s_msf, misc_taken.next())
            inverse_root(tD[:], rstd[:], signal=own)
            ofree.skip(QT * DEPTH)
            e.wait_ge(s_of, ofree.next())
            inverse_root(rt[:], rt[:])
            e.wait_ge(s_tab, 64)
            with L.loop(0, S_SV // 2) as i:
                for c in range(2):
                    for b in range(TB):
                        tiles.skip(1)
                        if b == TB - 1:
                            prep(c)
                        e.wait_ge(s_mmf, taken.next())
                        s = sv[:, b, bass.ds(i * 512 + c * 256, 256)]
                        e.activation(s, s, ACT.Gelu_apprx_tanh).then_inc(s_gel, gel.up())
            hi(wsph[:], wspr[:])
            for c in range(S_U):
                e.preload_act_table_set(LN_EXP)
                e.wait_ge(s_val, val.next())
                inverse_root(mv[:, 1:2], mv[:, 1:2])
                e.wait_ge(s_val, val.next())
                hi(svh[:, c, :], sv[:, c, :])
                for d in range(2):
                    tiles.skip(1)
                    if d:
                        prep(c % 2)
                    e.wait_ge(s_mmf, taken.next())
                    e.activation(us[:, 2 * c + d, :], us[:, 2 * c + d, :], ACT.Gelu_apprx_tanh).then_inc(s_fn, fn.up())
            for ct in range(KT):
                tiles.skip(1)
                taken.skip(1)
                e.wait_ge(s_val, val.next())
                hi(yh[:, ct, :], tD[:])
            with L.loop(0, S_SGU // 2) as i:
                tiles.skip(2)
                prep(0)
                e.wait_ge(s_mmf, taken.next(2))
                e.activation(tA[:, 0:T], tA[:, 0:T], ACT.Sigmoid).then_inc(s_fn, fn.up())
                e.activation(tB[:, 0:T], tB[:, 0:T], ACT.Sigmoid).then_inc(s_fn, fn.up())
                tiles.skip(2)
                prep(1)
                taken.skip(2)
            for h in range(RH):
                e.wait_ge(s_val, val.next())
                e.activation(dtab[:, h, :], dtab[:, h, :], ACT.Exp).then_inc(s_fn, fn.up())

            def v_hi(b):
                tiles.skip(1)
                e.wait_ge(s_mmf, taken.next())
                hi(rvh[:, b, :], sq[:, b // 2, DV * (b % 2):DV * (b % 2) + DV])

            def head_squares():
                misc_taken.skip(1)
                for d in range(2):
                    e.wait_ge(s_val, val.next())
                    e.activation(sq[:, d, :], (tC, tD)[d][:], ACT.Square).then_inc(s_fn, fn.up())

            def output_root():
                e.preload_act_table_set(LN_EXP)
                e.wait_ge(s_msf, misc_taken.next())
                inverse_root(sq[:, 0, :], sq[:, 1, :])

            for hd in range(RH):
                h = hd % 2
                tiles.skip(1)
                taken.skip(1)
                if hd:
                    head_squares()
                tiles.skip(1)
                taken.skip(1)
                prep(h)
                if hd:
                    output_root()
                for b, dst in ((0, rqh), (1, rkh)):
                    v_hi(b)
                    misc_taken.skip(1)
                    e.wait_ge(s_val, val.next())
                    hi(dst[:], tC[:])
                v_hi(2)
                v_hi(3)
                prep(1 - h)
                for mb in range(TB):
                    e.wait_ge(s_val, val.next())
                    hi(rph[:, mb, :], (tC, tD)[mb % 2][:])
                tiles.skip(2)
                prep(h)
                e.wait_ge(s_mmf, taken.next(2))
                for m in (2 * hd, 2 * hd + 1):
                    e.activation(og[:, m, :], og[:, m, :], ACT.Silu).then_inc(s_fn, fn.up())
            head_squares()
            output_root()
            with L.loop(0, S_AR // 2) as i:
                for c in range(2):
                    for d in range(2):
                        m = i * 4 + (2 * c + d)
                        e.wait_ge(s_og, ogs.next())
                        hi(tile(ogh, m), tile(og, m))
                        tiles.skip(1)
                        if d:
                            prep(c)
                        e.wait_ge(s_mmf, taken.next())
                        e.activation(tile(ar, m), tile(ar, m), ACT.Sigmoid).then_inc(s_fn, fn.up())
            with L.loop(0, S_RO // 2) as i:
                for c in range(2):
                    for d in range(2):
                        tiles.skip(1)
                        if d:
                            prep(c)
                        taken.skip(1)
                        e.wait_ge(s_val, val.next())
                        hi(tile(xh, i * 4 + (2 * c + d)), tD[:])
            with L.loop(0, S_OUT // 2) as i:
                for c in range(2):
                    for d in range(2):
                        tiles.skip(1)
                        if d:
                            prep(c)
                        e.wait_ge(s_sum, added.next())
                        e.wait_ge(s_mmf, taken.next())
                        square(tile(z, i * 4 + (2 * c + d)), d)
            e.preload_act_table_set(LN_EXP)
            e.wait_ge(s_msf, misc_taken.next())
            inverse_root(tD[:], rstd[:])
            for m in range(KT):
                e.wait_ge(s_sum, added.next())
                e.wait_ge(s_val, val.next())
                hi(xh[:, m, :], x[:, m, :], pars[:, B_GF + m:B_GF + m + 1])
                square(x[:, m, :], m % 2)
            e.preload_act_table_set(LN_EXP)
            e.wait_ge(s_msf, misc_taken.next())
            inverse_root(tD[:], rstd[:])
            def gated_conv(m, b0, c, cols=CH):
                for hf, src, dst in ((0, tA, tC), (4, tB, tD)):
                    tiles.skip(1)
                    e.wait_ge(s_mmf, taken.next())
                    e.activation(dst[:], src[:, 0:T], ACT.Identity, scale=col(pars, b0 + hf),
                                 bias=col(pars, b0 + (hf + 3))).then_inc(s_fn, fn.up())
                    if hf == 0:
                        e.wait_ge(s_val, val.next())
                        e.activation(tC[:], tC[:], ACT.Gelu_apprx_tanh).then_inc(s_fn, fn.up())
                prep(c, cols)
                e.wait_ge(s_val, val.next())
                hi(tile(acth, m), tD[:])

            with L.loop(0, S_UP // 2 - 1) as i:
                b0 = e.snap(i * 16)
                gated_conv(i * 2, b0 + B_CV, 0)
                gated_conv(i * 2 + 1, b0 + (B_CV + 8), 1)
            for c in range(2):
                gated_conv(FT - 2 + c, B_CV + 8 * (FT - 2 + c), c, HALF)

            def down2(m, d, more=True):
                if more:
                    prep(0, HALF, after_half=True)
                tiles.skip(1)
                if more:
                    prep(1, HALF)
                e.wait_ge(s_sum, added.next())
                e.wait_ge(s_mmf, taken.next())
                square(tile(z2, m), d)

            with L.loop(0, KT // 2 - 1) as i:
                down2(i * 2, 0)
                down2(i * 2 + 1, 1)
            down2(KT - 2, 0)
            down2(KT - 1, 1, more=False)
            e.preload_act_table_set(LN_EXP)
            e.wait_ge(s_msf, misc_taken.next())
            inverse_root(tD[:], rstd[:])

        @block.vector
        def _(e):
            L = Loops(e, "dve", strides)
            whi_in, w_out, tiles, taken = L.count(s_whi), L.count(s_w), L.count(s_mm), L.count(s_mmf)
            misc, misc_taken, fn, val = L.count(s_ms), L.count(s_msf), L.count(s_fn), L.count(s_val)
            in_out, sub, rot, own = L.count(s_in), L.count(s_sub), L.count(s_rot), L.count(s_do)
            zs, zero, qo, kvo, scores = (L.count(s) for s in (s_zs, s_zero, s_q, s_kv, s_s))
            mxs, ex, probs, pthi, ptlo = (L.count(s) for s in (s_m, s_e, s_p, s_pth, s_ptl))
            root, ogs, summed = L.count(s_root), L.count(s_og), L.count(s_acc)
            summed.skip(1)
            o_in, o_taken, gate, gel, par = (L.count(s) for s in (s_o, s_of, s_ga, s_gel, s_par))
            fin = L.count(s_fin)
            e.sem_inc(s_w, 2)
            e.sem_inc(s_mmf, 2)
            e.sem_inc(s_msf, 1)
            e.sem_inc(s_do, 1)
            w_out.skip(2)
            taken.skip(2)
            own.skip(1)
            misc_taken.skip(1)
            tiles.skip(1)
            TT, TS, STT = e.tensor_tensor, e.tensor_scalar, e.scalar_tensor_tensor

            def step(ins):
                ins.then_inc(s_do, own.up())
                e.wait_ge(s_do, own.now())

            def prep(slot, cols=CH):
                e.wait_ge(s_whi, whi_in.next())
                TT(wlo[:, slot, 0:cols], raw[:, slot, 0:cols], r32(whi[:, slot, 0:cols]), ALU.subtract).then_inc(s_w, w_out.up())

            def take(dst, bank, op_in=None):
                e.wait_ge(s_mm, tiles.next())
                TT(dst, mm[bank][:], rstd[:] if op_in is None else op_in, ALU.mult).then_inc(s_mmf, taken.up())

            def mean_square(n, dst):
                e.wait_ge(s_ms, misc.next())
                TS(dst, mi[:], 1.0 / n, EPS, ALU.mult, ALU.add).then_inc(s_msf, misc_taken.up())

            def input_norm(dst, zero=True):
                mean_square(D, dst)
                if zero:
                    e.memset(ssum[:], 0.0).then_inc(s_zs, zs.up())
                e.wait_ge(s_fn, fn.next())

            def lo(dst, src, hi_, out=None):
                e.wait_ge(s_fn, fn.next())
                told = out or sub
                TT(dst, src, r32(hi_), ALU.subtract).then_inc(told.sem, told.up())

            def in_lo(m, g):
                e.wait_ge(s_fn, fn.next())
                STT(tile(xl, m), tile(x, m), g, r32(tile(xh, m)), ALU.mult, ALU.subtract).then_inc(s_in, in_out.up())

            e.memset(ssum[:], 0.0).then_inc(s_zs, zs.up())
            e.wait_ge(s_x0, 32)
            prep(0)
            for k in range(KT):
                in_lo(k, pars[:, B_G0 + k:B_G0 + k + 1])
            prep(1)

            first = TAPS_U[0] + TAPS_U[1]
            taps = [(0, j) for j in range(first)]
            for t in range(VT - 1):
                more = TAPS - first
                taps += [tj for j in range(more) for tj in ((t, first + j), (t + 1, j))]
                first = more
            taps += [(VT - 1, j) for j in range(first, TAPS)]
            assert sorted(taps) == [(t, j) for t in range(VT) for j in range(TAPS)]

            def convolve(count):
                for t, j in taps[at[0]:at[0] + count]:
                    w = parl[:, A_CW + t * TAPS + j:A_CW + t * TAPS + j + 1]
                    a = apad[:, t, j:j + T]
                    if j == 0:
                        TS(y[:, t, :], a, w, parl[:, A_CB + t:A_CB + t + 1], ALU.mult, ALU.add).then_inc(s_do, own.up())
                    else:
                        e.wait_ge(s_do, own.now(own.n - tapped[t]))
                        STT(y[:, t, :], a, w, y[:, t, :], ALU.mult, ALU.add).then_inc(s_do, own.up())
                    tapped[t] = own.n
                at[0] += count

            with L.loop(0, DEPTH) as l:
                input_norm(ems[:], zero=False)
                at, tapped = [0], [0] * CT
                e.wait_ge(s_zero, zero.next(5))
                e.wait_ge(s_par, par.next(32))
                for c in range(L_UG):
                    if c == 0:
                        e.wait_ge(s_do, own.now())
                    take(tA[:, 0:T], 0)
                    take(tB[:, 0:T], 1)
                    prep(c % 2, CH if c < L_UG - L_KV else CH // 2)
                    e.wait_ge(s_fn, fn.next())
                    e.wait_ge(s_mmf, taken.now())
                    TT(apad[:, c, LEAD:PADW], tA[:, 0:T], tC[:], ALU.mult).then_inc(s_do, own.up())
                    e.wait_ge(s_do, own.now())
                    convolve(TAPS_U[c])
                kraw = pr[:, 0, 0:2, :].rearrange("p a b -> p (a b)")
                krot = pr[:, 0, 2:4, :].rearrange("p a b -> p (a b)")
                vval = pr[:, 1, 0:2, :].rearrange("p a b -> p (a b)")
                e.wait_ge(s_mm, tiles.next())
                e.tensor_copy(kraw, mm[0][:]).then_inc(s_mmf, taken.up())
                prep(0)
                take(vval, 1)
                e.wait_ge(s_ms, misc.next())
                step(STT(tB[:, 0:T], ems[:], HD * EPS, mi[:], ALU.mult, ALU.add))
                TS(tB[:, 0:T], tB[:, 0:T], 1.0 / HD, None, ALU.mult).then_inc(s_msf, misc_taken.up())
                convolve(TAPS_KV)
                e.wait_ge(s_root, root.next())
                STT(kraw, kraw, parl[:, A_KN:A_KN + 1], tC[:], ALU.mult, ALU.mult).then_inc(s_rot, rot.up())
                prep(1)
                e.wait_ge(s_rot, rot.now())
                TT(krot, kraw, rope1[:, 0, :], ALU.mult).then_inc(s_do, own.up())
                e.wait_ge(s_do, own.now())
                before = {QT: 8, QT + 1: TAPS_ATT[QT + 1]}
                for c in range(QT + 2):
                    if c == 0:
                        e.wait_ge(s_ms, misc.next())
                        TT(tC[:], mi[:], rope1[:, 1, :], ALU.mult).then_inc(s_msf, misc_taken.up())
                        e.wait_ge(s_msf, misc_taken.now())
                        TT(krot, krot, tC[:], ALU.add).then_inc(s_rot, rot.up())
                        e.wait_ge(s_rot, rot.now())
                    if c < QT:
                        e.wait_ge(s_ms, misc.next())
                        STT(tB[:, 0:T], ems[:], HD * EPS, mi[:], ALU.mult, ALU.add).then_inc(s_msf, misc_taken.up())
                    if c >= 2:
                        for h in range(2):
                            e.wait_ge(s_pth, pthi.next())
                            TT(ptl[:, h, :], spf[h][:, 0:896], r32(pth[:, h, :]), ALU.subtract).then_inc(s_ptl, ptlo.up())
                    if c < QT:
                        e.wait_ge(s_root, root.next())
                        tiles.skip(1)
                        if c:
                            e.wait_ge(s_q, qo.now())
                        STT(tD[:], mm[0][:], parl[:, A_QN:A_QN + 1], tC[:], ALU.mult, ALU.mult).then_inc(s_mmf, taken.up())
                        if c == 0:
                            scores.skip(2)
                            kf = (t[:, :, :].rearrange("p a t -> p (a t)") for t in (kl, kh))
                            lo(next(kf), spf[0], next(kf), kvo)
                            lo(vl[:, :, :, 64:128], spf[1][:, 0:T].rearrange("p (b k d) -> p b k d", b=TB, k=2),
                               vh[:, :, :, 64:128], kvo)
                        e.wait_ge(s_mmf, taken.now())
                        TT(tB[:, 0:T], tD[:], rope1[:, 0, :], ALU.mult).then_inc(s_do, own.up())
                        take(ga[:, c, :], 1)
                    else:
                        for d in range(2):
                            take(gb[2 * (c - QT) + d], d)
                            if d == 0:
                                convolve(before[c])
                    if c >= 2:
                        e.wait_ge(s_o, o_in.next())
                        e.wait_ge(s_ga, gate.next())
                        TT(ga[:, c - 2, :], ob[:], ga[:, c - 2, :], ALU.mult).then_inc(s_of, o_taken.up())
                    if 1 <= c <= QT:
                        for h in range(2):
                            e.wait_ge(s_s, scores.next())
                            L.park(s_idle)
                            head = 2 * (c - 1) + h
                            for n in range(TB):
                                w0 = P if n == 0 else 0
                                j = 4 * h + n
                                e.tensor_tensor_reduce(
                                    out=pr[:, h, n, w0:256], in0=sp[h][:, n, w0:256], in1=mask[:, w0:256],
                                    scale=1.0, scalar=parl[:, A_SINK + head:A_SINK + head + 1],
                                    op0=ALU.add, op1=ALU.max, accum_out=mx[:, j:j + 1]).then_inc(s_do, own.up())
                            e.wait_ge(s_do, own.now())
                            TS(ng[:, 4 * h:4 * h + 4], mx[:, 4 * h:4 * h + 4], -1.0, None,
                               ALU.mult).then_inc(s_m, mxs.up())
                    if c < QT:
                        e.wait_ge(s_ms, misc.next())
                        TT(tC[:], mi[:], rope1[:, 1, :], ALU.mult).then_inc(s_msf, misc_taken.up())
                        e.wait_ge(s_msf, misc_taken.now())
                        TT(tD[:], tB[:, 0:T], tC[:], ALU.add).then_inc(s_val, val.up())
                    for h in range(2):
                        if 1 <= c <= QT:
                            e.wait_ge(s_e, ex.next())
                            hs = slice(4 * h, 4 * h + 4)
                            step(TT(ls[:, hs], ls[:, hs], es[:, hs], ALU.add))
                            step(e.reciprocal(rl[:, hs], ls[:, hs]))
                            for n in range(TB):
                                p = pr[:, h, n, (P if n == 0 else 0):256]
                                last = TS(p, p, rl[:, 4 * h + n:4 * h + n + 1], None, ALU.mult)
                            last.then_inc(s_p, probs.up())
                        if h == 0 and c < QT:
                            convolve(2)
                    convolve(TAPS_ATT[c] - (2 if c < QT else before[c]))
                    if c < QT:
                        lo(ql[:, c % 2, :], tD[:], qh[:, c % 2, :], qo)
                    prep(c % 2)
                e.wait_ge(s_do, own.now())
                e.wait_ge(s_acc, summed.next(TAPS))
                step(TT(tA[:, 0:T], y[:, 0, :], y[:, 1, :], ALU.add))
                step(TT(tA[:, 0:T], tA[:, 0:T], y[:, 2, :], ALU.add))
                TT(tA[:, 0:T], tA[:, 0:T], y[:, 3, :], ALU.add).then_inc(s_rot, rot.up())
                e.memset(ssum[:], 0.0).then_inc(s_zs, zs.up())
                take(gb[4], 0)
                e.wait_ge(s_ms, misc.next())
                TS(tB[:, 0:T], mi[:], 1.0 / CONV_CH, None, ALU.mult).then_inc(s_msf, misc_taken.up())
                e.wait_ge(s_msf, misc_taken.now())
                for t in range(CT):
                    TT(y[:, t, :], y[:, t, :], tB[:, 0:T], ALU.subtract).then_inc(s_val, val.up())
                e.wait_ge(s_fn, fn.next(4))
                step(TT(tA[:, 0:T], tA[:, 0:T], tC[:], ALU.add))
                step(TT(tA[:, 0:T], tA[:, 0:T], tD[:], ALU.add))
                TT(tA[:, 0:T], tA[:, 0:T], sq[:, 0, :], ALU.add).then_inc(s_rot, rot.up())
                take(gb[5], 1)
                prep(0)
                mean_square(CONV_CH, tB[:, 0:T])
                e.wait_ge(s_fn, fn.next())
                for t in range(CT):
                    TT(y[:, t, :], y[:, t, :], tC[:], ALU.mult).then_inc(s_val, val.up())
                take(gb[6], 0)
                for t in range(CT):
                    lo(cvl[:, t, :], y[:, t, :], cvh[:, t, :])
                take(gb[7], 1)
                prep(1)
                merged = (tD, tB)
                for m in range(KT + 1):
                    if m < KT:
                        if m > 1:
                            e.wait_ge(s_sub, sub.now())
                        e.wait_ge(s_ga, gate.next())
                        branch = (tC, tA)[m % 2][:, 0:T]
                        take(branch, m % 2, gb[m])
                        e.wait_ge(s_mmf, taken.now())
                        TT(merged[m % 2][:, 0:T], branch, ga[:, m, :], ALU.add).then_inc(s_val, val.up())
                    if m:
                        lo(ml[:, m - 1, :], merged[(m - 1) % 2][:, 0:T], mh[:, m - 1, :])
                    if m in (3, 7):
                        prep(m // 4)
                with L.loop(0, L_OUT // 2) as i:
                    for c in range(2):
                        for d in range(2):
                            m = i * 4 + (2 * c + d)
                            e.wait_ge(s_mm, tiles.next())
                            TT(tile(x, m), mm[d][:], tile(x, m), ALU.add).then_inc(s_mmf, taken.up())
                            in_lo(m, col(parl, m + A_GF))
                            if d:
                                prep(c)
                input_norm(tD[:])
                L.park(s_idle)
                def gated(m, c, cols=CH):
                    take(tA[:, 0:T], 0)
                    take(tB[:, 0:T], 1)
                    prep(c, cols)
                    e.wait_ge(s_fn, fn.next())
                    e.wait_ge(s_mmf, taken.now())
                    TT(tD[:], tC[:], tB[:, 0:T], ALU.mult).then_inc(s_val, val.up())
                    lo(tile(actl, m), tD[:], tile(acth, m))

                with L.loop(0, L_GU // 2 - 1) as i:
                    gated(i * 2, 0)
                    gated(i * 2 + 1, 1)
                gated(FT - 2, 0, HALF)
                gated(FT - 1, 1, HALF)

                def down(m, d, cols=HALF):
                    prep(0, cols)
                    e.wait_ge(s_mm, tiles.next())
                    TT(tile(x, m), mm[d][:], tile(x, m), ALU.add).then_inc(s_mmf, taken.up())
                    in_lo(m, col(parl, m + A_GN))
                    prep(1, cols)

                with L.loop(0, KT // 2 - 1) as i:
                    down(i * 2, 0)
                    down(i * 2 + 1, 1)
                down(KT - 2, 0)
                down(KT - 1, 1, CH)

            v, zz, s1, s2, pz, tmp = (sm[:, j, :] for j in range(6))
            logit = pars[:, B_DL:B_DL + 8]
            step(TS(tmp, logit, -1.0, None, ALU.mult))
            TT(v, logit, tmp, ALU.max).then_inc(s_val, val.up())
            e.wait_ge(s_fn, fn.next())
            step(TS(s2, zz, 2.0, None, ALU.add))
            step(e.reciprocal(s1, s2))
            step(TT(s1, s1, zz, ALU.mult))
            step(TT(s2, s1, s1, ALU.mult))
            step(TS(pz, s2, 1.0 / 17, 1.0 / 15, ALU.mult, ALU.add))
            for odd in (13, 11, 9, 7, 5, 3, 1):
                step(TT(pz, pz, s2, ALU.mult))
                step(TS(pz, pz, 1.0 / odd, None, ALU.add))
            step(TT(pz, pz, s1, ALU.mult))
            step(TS(tmp, logit, 0.0, None, ALU.min))
            STT(lg[:], pz, -2.0, tmp, ALU.mult, ALU.add).then_inc(s_do, own.up())

            mean_square(D, tD[:])
            e.wait_ge(s_o, o_in.next())
            TS(rt[:], ob[:, 0:TB], 1.0 / D, EPS, ALU.mult, ALU.add).then_inc(s_of, o_taken.up())
            e.memset(ssum[:], 0.0).then_inc(s_zs, zs.up())
            e.wait_ge(s_fn, fn.next())
            with L.loop(0, S_SV // 2) as i:
                for c in range(2):
                    for b in range(TB):
                        e.wait_ge(s_mm, tiles.next())
                        TS(sv[:, b, bass.ds(i * 512 + c * 256, 256)], mm[b % 2][:, 0:256],
                           rt[:, b:b + 1], None, ALU.mult).then_inc(s_mmf, taken.up())
                    prep(c)
            e.wait_ge(s_tab, 64)
            lo(wspl[:], wspr[:], wsph[:])
            e.wait_ge(s_gel, gel.next(4 * S_SV))
            for c in range(S_U):
                e.bn_stats(st[:, 0, :], sv[:, c, 0:512]).then_inc(s_do, own.up())
                step(e.bn_stats(st[:, 1, :], sv[:, c, 512:1024]))
                step(e.bn_aggr(mv[:], st[:, :, :].rearrange("p a b -> p (a b)")))
                TS(mv[:, 1:2], mv[:, 1:2], EPS, None, ALU.add).then_inc(s_val, val.up())
                take(us[:, 2 * c, :], 0)
                e.wait_ge(s_fn, fn.next(3 if c else 1))
                step(TS(sv[:, c, :], sv[:, c, :], mv[:, 0:1], mv[:, 1:2], ALU.subtract, ALU.mult))
                step(TT(sv[:, c, :], sv[:, c, :], gtab[:], ALU.mult))
                TT(sv[:, c, :], sv[:, c, :], btab[:], ALU.add).then_inc(s_val, val.up())
                lo(svl[:, c, :], sv[:, c, :], svh[:, c, :])
                take(us[:, 2 * c + 1, :], 1)
                prep(c % 2)
            e.wait_ge(s_fn, fn.next(2))
            for ct in range(KT):
                e.wait_ge(s_mm, tiles.next())
                bias = bsp[:, ct // 2, :].rearrange("p (a q) -> p a q", a=1).broadcast_to([P, TB, P])
                TT(tA[:, 0:T].rearrange("p (a q) -> p a q", a=TB),
                                mm[ct % 2][:].rearrange("p (a q) -> p a q", a=TB), bias, ALU.add).then_inc(s_mmf, taken.up())
                e.wait_ge(s_mmf, taken.now())
                TT(tD[:], tA[:, 0:T], us[:, ct, :], ALU.mult).then_inc(s_val, val.up())
                lo(yl[:, ct, :], tD[:], yh[:, ct, :])
            with L.loop(0, S_SGU // 2) as i:
                take(tA[:, 0:T], 0)
                take(tB[:, 0:T], 1)
                prep(0)
                e.wait_ge(s_fn, fn.next(2))
                for d in range(2):
                    take(tile(msgu, i * 2 + d), d, (tA, tB)[d][:, 0:T])
                prep(1)
            e.wait_ge(s_tab2, 32)
            for h in range(RH):
                step(TS(dtab[:, h, :], dist[:, 0, :], lg[:, h:h + 1], None, ALU.mult))
                STT(dtab[:, h, :], dist[:, 1, :], lg[:, RH + h:RH + h + 1], dtab[:, h, :], ALU.mult, ALU.add).then_inc(s_val, val.up())
            e.wait_ge(s_fn, fn.next(RH))

            def v_take(b):
                e.wait_ge(s_mm, tiles.next())
                vt = sq[:, b // 2, DV * (b % 2):DV * (b % 2) + DV]
                TS(vt, mm[b % 2][:, 0:DV], rt[:, b:b + 1], None, ALU.mult).then_inc(s_mmf, taken.up())
                lo(rvl[:, b, :], vt, rvh[:, b, :])

            def rotate(src, scale, dst_hi, dst_lo):
                STT(tC[:], src[:, 0:T], scale, rope2[:, 0, :], ALU.mult, ALU.mult).then_inc(s_do, own.up())
                e.wait_ge(s_ms, misc.next())
                STT(tD[:], mi[:], scale, rope2[:, 1, :], ALU.mult, ALU.mult).then_inc(s_msf, misc_taken.up())
                e.wait_ge(s_msf, misc_taken.now())
                TT(tC[:], tC[:], tD[:], ALU.add).then_inc(s_val, val.up())
                lo(dst_lo[:], tC[:], dst_hi[:], qo)

            def centre():
                e.wait_ge(s_ms, misc.next())
                TS(sq[:, 1, :], mi[:], 1.0 / DV, None, ALU.mult).then_inc(s_msf, misc_taken.up())
                e.wait_ge(s_msf, misc_taken.now())
                TT(tC[:], tC[:], sq[:, 1, :], ALU.subtract).then_inc(s_val, val.up())
                TT(tD[:], tD[:], sq[:, 1, :], ALU.subtract).then_inc(s_val, val.up())
                e.wait_ge(s_fn, fn.next(2))
                TT(sq[:, 0, :], sq[:, 0, :], sq[:, 1, :], ALU.add).then_inc(s_rot, rot.up())

            def gate_output(hd):
                mean_square(DV, sq[:, 0, :])
                e.wait_ge(s_fn, fn.next())
                for t in (tC, tD):
                    TT(t[:], t[:], sq[:, 1, :], ALU.mult).then_inc(s_do, own.up())
                for d, t in ((0, tC), (1, tD)):
                    e.wait_ge(s_do, own.now(1 - d))
                    m = 2 * hd + d
                    TT(og[:, m, :], t[:], og[:, m, :], ALU.mult).then_inc(s_og, ogs.up())

            for hd in range(RH):
                h = hd % 2
                take(tA[:, 0:T], 0)
                if hd:
                    centre()
                take(tB[:, 0:T], 1)
                if hd:
                    gate_output(hd - 1)
                    e.wait_ge(s_og, ogs.now())
                prep(h)
                v_take(0)
                rotate(tA, 1.0, rqh, rql)
                v_take(1)
                rotate(tB, float(DK) ** -0.5, rkh, rkl)
                v_take(2)
                v_take(3)
                prep(1 - h)
                for mb in range(TB):
                    e.wait_ge(s_s, scores.next())
                    t = (tC, tD)[mb % 2]
                    win = (TB - 1 - mb) * P
                    TT(t[:], spf[mb // 2][:, T * (mb % 2):T * (mb % 2) + T],
                       dtab[:, hd, win:win + T], ALU.mult).then_inc(s_val, val.up())
                    lo(rpl[:, mb, :], t[:], rph[:, mb, :])
                take(og[:, 2 * hd, :], 0)
                take(og[:, 2 * hd + 1, :], 1)
                prep(h)
                e.wait_ge(s_fn, fn.next(2))
                e.wait_ge(s_o, o_in.next())
                e.tensor_copy(tC[:], ob[:]).then_inc(s_do, own.up())
                e.wait_ge(s_o, o_in.next())
                step(e.tensor_copy(tD[:], spf[0][:, 0:T]))
                TT(sq[:, 0, :], tC[:], tD[:], ALU.add).then_inc(s_rot, rot.up())
            centre()
            gate_output(RH - 1)
            with L.loop(0, S_AR // 2) as i:
                for c in range(2):
                    for d in range(2):
                        m = i * 4 + (2 * c + d)
                        lo(tile(ogl, m), tile(og, m), tile(ogh, m))
                        take(tile(ar, m), d)
                        if d:
                            prep(c)
                        e.wait_ge(s_fn, fn.next())
            with L.loop(0, S_RO // 2) as i:
                for c in range(2):
                    for d in range(2):
                        m = i * 4 + (2 * c + d)
                        take(tA[:, 0:T], d, tile(ar, m))
                        e.wait_ge(s_mmf, taken.now())
                        TT(tD[:], tA[:, 0:T], tile(msgu, m), ALU.add).then_inc(s_val, val.up())
                        if d:
                            prep(c)
                        lo(tile(xl, m), tD[:], tile(xh, m), in_out)
            with L.loop(0, S_OUT // 2) as i:
                for c in range(2):
                    for d in range(2):
                        e.wait_ge(s_mm, tiles.next())
                        e.tensor_copy(tile(z, i * 4 + (2 * c + d)), mm[d][:]).then_inc(s_mmf, taken.up())
                    prep(c)
            e.wait_ge(s_mmf, taken.now())
            input_norm(tD[:])
            for m in range(KT + 1):
                if m < KT:
                    if m > 1:
                        e.wait_ge(s_in, in_out.now())
                    t = (tA, tC)[m % 2][:, 0:T]
                    step(STT(t, z[:, m, :], pars[:, B_GP + m:B_GP + m + 1], rstd[:], ALU.mult, ALU.mult))
                    TT(x[:, m, :], x[:, m, :], t, ALU.add).then_inc(s_val, val.up())
                if m:
                    in_lo(m - 1, pars[:, B_GF + m - 1:B_GF + m])
            for t in (tA, tB):
                e.memset(t[:, 0:1], 0.0).then_inc(s_do, own.up())
                e.memset(t[:, T + 1:T + 2], 0.0).then_inc(s_do, own.up())
            input_norm(tD[:])
            def gated_conv(m, b0, c, cols=CH):
                for hf, src, dst in ((0, tA, tC), (4, tB, tD)):
                    take(src[:, 1:T + 1], hf // 4)
                    e.wait_ge(s_fn, fn.next(2 if hf else 1))
                    e.wait_ge(s_mmf, taken.now())
                    step(STT(dst[:], src[:, 1:T + 1], col(pars, b0 + (hf + 1)), dst[:], ALU.mult, ALU.add))
                    last = STT(dst[:], src[:, 2:T + 2], col(pars, b0 + (hf + 2)), dst[:], ALU.mult, ALU.add)
                    if hf:
                        last.then_inc(s_do, own.up())
                    else:
                        last.then_inc(s_val, val.up())
                e.wait_ge(s_do, own.now())
                TT(tD[:], tC[:], tD[:], ALU.mult).then_inc(s_val, val.up())
                prep(c, cols)
                lo(tile(actl, m), tD[:], tile(acth, m))

            with L.loop(0, S_UP // 2 - 1) as i:
                b0 = e.snap(i * 16)
                gated_conv(i * 2, b0 + B_CV, 0)
                gated_conv(i * 2 + 1, b0 + (B_CV + 8), 1)
            for c in range(2):
                gated_conv(FT - 2 + c, B_CV + 8 * (FT - 2 + c), c, HALF)

            def down2(m, d, more=True):
                if more:
                    prep(0, HALF)
                e.wait_ge(s_mm, tiles.next())
                e.tensor_copy(tile(z2, m), mm[d][:]).then_inc(s_mmf, taken.up())
                if more:
                    prep(1, HALF)

            with L.loop(0, KT // 2 - 1) as i:
                down2(i * 2, 0)
                down2(i * 2 + 1, 1)
            down2(KT - 2, 0)
            down2(KT - 1, 1, more=False)
            mean_square(D, tD[:])
            e.wait_ge(s_mmf, taken.now())
            e.wait_ge(s_fn, fn.next())
            for m in range(KT):
                if m:
                    e.wait_ge(s_fin, fin.now())
                step(STT(tA[:, 0:T], z2[:, m, :], pars[:, B_GO + m:B_GO + m + 1], rstd[:], ALU.mult, ALU.mult))
                TT(x[:, m, :], x[:, m, :], tA[:, 0:T], ALU.add).then_inc(s_fin, fin.up())

        @block.tensor
        def _(e):
            L = Loops(e, "pe", strides)
            w_in, tiles, half, taken = L.count(s_w), L.count(s_mm), L.count(s_half), L.count(s_mmf)
            misc, misc_taken, inp, sub, rot = (L.count(s) for s in (s_ms, s_msf, s_in, s_sub, s_rot))
            sqq, added, q_in, kv_in, scores = (L.count(s) for s in (s_sqq, s_sum, s_q, s_kv, s_s))
            probs, pt, ptlo, o_out = (L.count(s) for s in (s_p, s_pt, s_ptl, s_o))
            e.sem_inc(s_mm, 1)
            w_in.skip(2)
            tiles.skip(1)
            added.skip(2)
            MM = e.matmul

            def mm3(out, ah, al, bh, bl, first, last, **kw):
                MM(out, ah, bh, start=first, stop=False, **kw)
                MM(out, ah, bl, start=False, stop=False, **kw)
                return MM(out, al, bh, start=False, stop=last, **kw)

            def product(bank, slot, at, hi_, lo_, ks, ready=None, first=True, last=True):
                for j, k in enumerate(ks):
                    if ready is not None:
                        e.wait_ge(ready.sem, ready.next())
                    a = slice((at + j) * P, (at + j + 1) * P)
                    ins = mm3(mm[bank][:], whi[:, slot, a], wlo[:, slot, a], hi_[:, k, :], lo_[:, k, :],
                              first and j == 0, last and j == len(ks) - 1)
                return ins

            def out_tile(bank, slot, at, hi_, lo_, n_k, ready=None):
                e.wait_ge(s_mmf, taken.next())
                product(bank, slot, at, hi_, lo_, range(n_k), ready).then_inc(s_mm, tiles.up())

            def small(lhs, rhs, src=None):
                if src is not None:
                    e.wait_ge(src.sem, src.next())
                e.wait_ge(s_msf, misc_taken.next())
                MM(mi[:], lhs, rhs, start=True, stop=True).then_inc(s_ms, misc.up())

            def token_sums():
                e.wait_ge(s_cst, 16)
                e.wait_ge(s_sum, added.next(KT))
                small(ones, ssum[:])

            def pair(hi_, lo_, ready=None, norm=False):
                for c in range(2):
                    e.wait_ge(s_w, w_in.next())
                    for d in range(2):
                        out_tile(d, c, KT * d, hi_, lo_, KT, ready if c == d == 0 else None)
                        if norm and c == d == 0:
                            token_sums()

            def down():

                def two(ready):
                    for d in range(2):
                        e.wait_ge(s_w, w_in.next())
                        e.wait_ge(s_mmf, taken.next())
                        product(d, 0, 0, acth, actl, range(FT // 2), None if d else ready, last=False).then_inc(s_half, half.up())
                        e.wait_ge(s_w, w_in.next())
                        product(d, 1, 0, acth, actl, range(FT // 2, FT), None if d else ready, first=False).then_inc(s_mm, tiles.up())

                two(sub)
                with L.loop(1, KT // 2):
                    two(None)

            def attend(s, h):
                a = slice(64 * h, 64 * h + 64)
                for n in range(TB):
                    k0 = max(n - 1, 0) * P
                    qs = slice(n * P, (n + 1) * P)
                    ks = slice(k0, (n + 1) * P)
                    ins = mm3(sp[h][:, n, (P if n == 0 else 0):256], qh[a, s % 2, qs], ql[a, s % 2, qs],
                              kh[a, s // 4, ks], kl[a, s // 4, ks], True, True)
                ins.then_inc(s_s, scores.up())

            def turn(h):
                e.wait_ge(s_p, probs.next())
                for j in range(TB):
                    ins = e.transpose(spf[h][:, 256 * j:256 * j + P], pr[:, h, j, P:256], ident)
                    if j + 1 < TB:
                        ins = e.transpose(spf[h][:, 256 * j + P:256 * j + 256], pr[:, h, j + 1, 0:P], ident)
                ins.then_inc(s_pt, pt.up())

            def weigh(s):
                e.wait_ge(s_ptl, ptlo.next(2))
                for h in range(2):
                    for j in range(TB):
                        n = 2 * P if j + 1 < TB else P
                        v = slice(64 - 64 * h, 192 - 64 * h)
                        cs = slice(256 * j, 256 * j + n)
                        ins = mm3(ob[:, j * P:j * P + n], vh[:, j, s // 4, v], vl[:, j, s // 4, v],
                                  pth[:, h, cs], ptl[:, h, cs], h == j == 0, h == 1 and j == TB - 1,
                                  skip_group_check=True)
                ins.then_inc(s_o, o_out.up())

            with L.loop(0, DEPTH) as l:
                pair(xh, xl, inp, norm=True)
                with L.loop(1, L_UG // 2):
                    pair(xh, xl)
                e.wait_ge(s_w, w_in.next())
                out_tile(0, 0, 0, xh, xl, KT)
                e.wait_ge(s_w, w_in.next())
                out_tile(1, 1, 0, xh, xl, KT)
                small(bd, sq[:, 1, :], sqq)
                for c in range(QT + 2):
                    e.wait_ge(s_w, w_in.next())
                    out_tile(0, c % 2, 0, xh, xl, KT)
                    if c == 0:
                        small(rot1, pr[:, 0, 0:2, :].rearrange("p a b -> p (a b)"), rot)
                    if c >= 2:
                        turn(0)
                        turn(1)
                    if c < QT:
                        small(bd, sq[:, 0, :], sqq)
                    out_tile(1, c % 2, KT, xh, xl, KT)
                    if c == 0:
                        e.wait_ge(s_rot, rot.next())
                        for kv in range(2):
                            sel = cst[:, C_SEL + kv * P:C_SEL + (kv + 1) * P]
                            ins = MM(spf[0][:, kv * T:(kv + 1) * T], sel,
                                     pr[:, 0, 2:4, :].rearrange("p a b -> p (a b)"), start=True, stop=True)
                        ins.then_inc(s_s, scores.up())
                        for b in range(TB):
                            ins = e.transpose(spf[1][:, b * P:(b + 1) * P],
                                              pr[:, 1, b // 2, (b % 2) * P:(b % 2) * P + P], ident)
                        ins.then_inc(s_s, scores.up())
                    if c >= 2:
                        weigh(c - 2)
                    if 1 <= c <= QT:
                        e.wait_ge(s_q, q_in.next())
                        if c == 1:
                            e.wait_ge(s_kv, kv_in.next(2))
                        attend(c - 1, 0)
                        attend(c - 1, 1)
                    if c < QT:
                        e.wait_ge(s_mmf, taken.now(-1))
                        small(rot1, tD[:])
                e.wait_ge(s_w, w_in.next())
                out_tile(0, 0, 0, xh, xl, KT)
                small(ones, tA[:, 0:T], rot)
                out_tile(1, 0, KT, xh, xl, KT)
                small(ones, tA[:, 0:T], rot)
                e.wait_ge(s_w, w_in.next())
                out_tile(0, 1, 0, xh, xl, KT)
                out_tile(1, 1, KT, xh, xl, KT)
                for m in range(KT):
                    if m % 4 == 0:
                        e.wait_ge(s_w, w_in.next())
                    out_tile(m % 2, m // 4, CT * (m % 4), cvh, cvl, CT, None if m else sub)
                pair(mh, ml, sub)
                with L.loop(1, L_OUT // 2):
                    pair(mh, ml)
                pair(xh, xl, inp, norm=True)
                with L.loop(1, L_GU // 2):
                    pair(xh, xl)
                down()

            def token_major(slot, bank, b, ready=None):
                e.wait_ge(s_mmf, taken.next())
                ts = slice(b * P, (b + 1) * P)
                for k in range(KT):
                    if ready is not None:
                        e.wait_ge(ready.sem, ready.next())
                    ws = slice(256 * k, 256 * k + 256)
                    ins = mm3(mm[bank][:, 0:256], xh[:, k, ts], xl[:, k, ts], whi[:, slot, ws], wlo[:, slot, ws],
                              k == 0, k == KT - 1)
                ins.then_inc(s_mm, tiles.up())

            e.wait_ge(s_w, w_in.next())
            token_major(0, 0, 0, inp)
            token_sums()
            for b in range(TB):
                ins = MM(ob[:, b:b + 1], ssum[:, b * P:(b + 1) * P], ones[:, 0:1], start=True, stop=True)
            ins.then_inc(s_o, o_out.up())
            for b in range(1, TB):
                token_major(0, b % 2, b)
            e.wait_ge(s_w, w_in.next())
            for b in range(TB):
                token_major(1, b % 2, b)
            with L.loop(1, S_SV // 2):
                for c in range(2):
                    e.wait_ge(s_w, w_in.next())
                    for b in range(TB):
                        token_major(c, b % 2, b)
            with L.loop(0, S_U // 2):
                pair(xh, xl)
            e.wait_ge(s_sub, sub.next(1 + TB))
            for ct in range(KT):
                e.wait_ge(s_mmf, taken.next())
                for n in range(TB):
                    ins = mm3(mm[ct % 2][:, n * P:(n + 1) * P], svh[:, n, ct * P:(ct + 1) * P],
                              svl[:, n, ct * P:(ct + 1) * P], wsph[:, ct // 2, :], wspl[:, ct // 2, :], True, True)
                ins.then_inc(s_mm, tiles.up())

            def gate_and_out(ready):
                e.wait_ge(s_w, w_in.next())
                out_tile(0, 0, 0, xh, xl, KT)
                out_tile(1, 0, KT, xh, xl, KT)
                e.wait_ge(s_w, w_in.next())
                out_tile(0, 1, 0, yh, yl, KT, ready)
                out_tile(1, 1, KT, yh, yl, KT)

            gate_and_out(sub)
            with L.loop(1, S_SGU // 2):
                gate_and_out(None)

            def retain(hd):
                h = hd % 2
                e.wait_ge(s_w, w_in.next())
                out_tile(0, h, 0, xh, xl, KT)
                if hd:
                    small(ones, sq[:, 0, :], rot)
                out_tile(1, h, KT, xh, xl, KT)
                if hd:
                    small(ones, sq[:, 0, :], rot)
                e.wait_ge(s_w, w_in.next())
                token_major(1 - h, 0, 0)
                small(rot2, tA[:, 0:T])
                token_major(1 - h, 1, 1)
                small(rot2, tB[:, 0:T])
                token_major(1 - h, 0, 2)
                token_major(1 - h, 1, 3)
                e.wait_ge(s_q, q_in.next(2))
                for mb in range(TB):
                    cs = slice(mb * P, (mb + 1) * P)
                    mm3(spf[mb // 2][:, T * (mb % 2):T * (mb % 2) + T], rkh[:, cs], rkl[:, cs],
                                      rqh[:], rql[:], True, True).then_inc(s_s, scores.up())
                e.wait_ge(s_w, w_in.next())
                out_tile(0, h, 0, xh, xl, KT)
                out_tile(1, h, KT, xh, xl, KT)
                e.wait_ge(s_sub, sub.next(2 * TB))
                for d, dst in ((0, ob[:]), (1, spf[0][:, 0:T])):
                    for mb in range(TB):
                        cs = slice(d * P, (d + 1) * P)
                        ins = mm3(dst, rvh[:, mb, cs], rvl[:, mb, cs], rph[:, mb, :], rpl[:, mb, :],
                                  mb == 0, mb == TB - 1)
                    ins.then_inc(s_o, o_out.up())

            for hd in range(RH):
                retain(hd)
            small(ones, sq[:, 0, :], rot)
            small(ones, sq[:, 0, :], rot)
            with L.loop(0, S_AR // 2):
                pair(xh, xl)
            pair(ogh, ogl, sub)
            with L.loop(1, S_RO // 2):
                pair(ogh, ogl)
            pair(xh, xl, inp)
            with L.loop(1, S_OUT // 2):
                pair(xh, xl)
            token_sums()
            pair(xh, xl, inp, norm=True)
            with L.loop(1, S_UP // 2):
                pair(xh, xl)
            down()
            token_sums()



def constants():
    c = np.zeros((P, C_N), np.float32)
    c[:, C_ID:C_ID + P] = np.eye(P)
    c[:, C_ONE:C_ONE + P] = 1.0
    i = np.arange(P)
    c[:, C_BD:C_BD + P] = i[:, None] // HD == i[None, :] // HD
    half = ROT // 2
    for h in range(2):
        for d in range(half):
            c[h * HD + d + half, C_ROT1 + h * HD + d] = -1.0
            c[h * HD + d, C_ROT1 + h * HD + d + half] = 1.0
    for kv in range(2):
        for d in range(P):
            c[kv * HD + d % HD, C_SEL + kv * P + d] = 1.0
    for d in range(DK // 2):
        c[d + DK // 2, C_ROT2 + d] = -1.0
        c[d, C_ROT2 + d + DK // 2] = 1.0
    j = np.arange(256)
    rel = i[:, None] + P - j[None, :]
    c[:, C_MASK:C_MASK + 256] = np.where((rel >= 0) & (rel < P), 0.0, -1e30)
    return c


def rope_tables(theta, rot, width):
    half = rot // 2
    inv = (np.float32(theta) ** (-np.arange(0, rot, 2, dtype=np.float32) / np.float32(rot))).astype(np.float32)
    ang = (np.arange(T, dtype=np.float32)[:, None] * inv[None, :]).astype(np.float32)
    t = np.zeros((P, 2, T), np.float32)
    t[:, 0] = 1.0
    for base in range(0, P, width):
        for d in range(half):
            for r in (base + d, base + d + half):
                t[r, 0] = np.cos(ang[:, d])
                t[r, 1] = np.sin(ang[:, d])
    return t


def distances():
    d = np.arange(DWIN)[None, :] - (TB - 1) * P - np.arange(P)[:, None]
    return np.stack([np.maximum(d, 0), np.maximum(-d, 0)], 1).astype(np.float32)


def kernel(**inputs):
    import concourse.bacc as bacc
    from concourse.bass_utils import run_bass_kernel_spmd as run

    a = {k: np.asarray(v) for k, v in inputs.items()}
    W = np.zeros((N_CHUNKS, P, CH), np.float32)
    at = [0]

    def tiles_chunk(*tiles):
        c = 0
        for m, c0 in tiles:
            kt = m.shape[0] // P
            W[at[0], :, c:c + kt * P] = m[:, c0:c0 + P].reshape(kt, P, P).transpose(1, 0, 2).reshape(P, kt * P)
            c += kt * P
        at[0] += 1

    def columns_chunk(m, c0):
        W[at[0]] = m[:, c0:c0 + 256].reshape(KT, P, 256).transpose(1, 0, 2).reshape(P, CH)
        at[0] += 1

    def all_tiles(m):
        for c in range(0, KT, 2):
            tiles_chunk((m, c * P), (m, (c + 1) * P))

    def up_chunks(m):
        for t in range(FT):
            tiles_chunk((m, t * P), (m, FF + t * P))

    def down_chunks(m):
        for c in range(KT):
            for h in range(2):
                tiles_chunk((m[h * HALF:(h + 1) * HALF], c * P))

    parl = np.zeros((DEPTH, P, A_N), np.float32)
    pars = np.zeros((P, B_N), np.float32)
    by_tile = lambda v: v.reshape(-1, P).T
    q_w, kv_w = HEADS * HD, KV_HEADS * HD
    u0 = q_w + 2 * kv_w
    ga0 = u0 + 2 * CONV_CH
    for l in range(DEPTH):
        w = a["w_in"][l]
        for t in range(CT):
            tiles_chunk((w, u0 + t * P), (w, u0 + CONV_CH + t * P))
        tiles_chunk((w, q_w))
        tiles_chunk((w, q_w + kv_w))
        for t in range(QT):
            tiles_chunk((w, t * P), (w, ga0 + t * P))
        all_tiles(w[:, ga0 + D:])
        for t in range(0, KT, 4):
            tiles_chunk(*((a["w_conv_out"][l], (t + d) * P) for d in range(4)))
        all_tiles(a["w_out"][l])
        up_chunks(a["w_gate_up"][l])
        down_chunks(a["w_down"][l])
        p = parl[l]
        p[:, A_QN] = np.tile(a["q_norm"][l], 2)
        p[:, A_KN] = np.tile(a["k_norm"][l], 2)
        p[:, A_SINK:A_SINK + HEADS] = np.broadcast_to(a["sinks"][l], (P, HEADS))
        p[:, A_CW:A_CW + CT * TAPS] = a["conv_w"][l].reshape(TAPS, CT, P).transpose(2, 1, 0).reshape(P, CT * TAPS)
        p[:, A_CB:A_CB + CT] = by_tile(a["conv_b"][l])
        p[:, A_LG:A_LG + CT] = by_tile(a["conv_ln_g"][l])
        p[:, A_LB:A_LB + CT] = by_tile(a["conv_ln_b"][l])
        p[:, A_GF:A_GF + KT] = by_tile(a["norm_ffn"][l])
        p[:, A_GN:A_GN + KT] = by_tile(a["norm_mix"][l + 1] if l + 1 < DEPTH else a["g_pre_mix_2"])
    w = a["w_in_2"]
    offs = np.cumsum([0, RH * DK, RH * DK, RH * DV, RH * DV, D, D, D])
    q0, k0, v0, g0, us0, sv0, ar0, as0 = (int(o) for o in offs)
    for c in range(S_SV):
        columns_chunk(w, sv0 + 256 * c)
    for t in range(0, KT, 2):
        tiles_chunk((w, us0 + t * P), (w, us0 + (t + 1) * P))
    for t in range(0, KT, 2):
        tiles_chunk((w, as0 + t * P), (w, as0 + (t + 1) * P))
        tiles_chunk((a["w_sgu_o_2"], t * P), (a["w_sgu_o_2"], (t + 1) * P))
    for h in range(RH):
        tiles_chunk((w, q0 + h * DK), (w, k0 + h * DK))
        columns_chunk(w, v0 + h * DV)
        tiles_chunk((w, g0 + h * DV), (w, g0 + h * DV + P))
    all_tiles(w[:, ar0:ar0 + D])
    all_tiles(a["w_ret_o_2"])
    all_tiles(a["w_out_2"])
    up_chunks(a["w_up_2"])
    down_chunks(a["w_down_2"])
    assert at[0] == N_CHUNKS
    pars[:, B_GP:B_GP + KT] = by_tile(a["g_post_mix_2"])
    pars[:, B_GF:B_GF + KT] = by_tile(a["g_pre_ffn_2"])
    pars[:, B_GO:B_GO + KT] = by_tile(a["g_post_ffn_2"])
    pars[:, B_G0:B_G0 + KT] = by_tile(a["norm_mix"][0])
    pars[:, B_DL:B_DL + 2 * RH] = np.broadcast_to(a["ret_decay_logit_2"].reshape(-1), (P, 2 * RH))
    cv = np.concatenate([a["conv_w_2"], a["conv_b_2"][None]], 0)
    pars[:, B_CV:] = cv.reshape(4, 2, FT, P).transpose(3, 2, 1, 0).reshape(P, 8 * FT)
    sgt = np.zeros((P, 2 * D + 2 * SGU_G * P), np.float32)
    sgt[:, 0:D] = np.broadcast_to(a["sgu_ln_g_2"], (P, D))
    sgt[:, D:2 * D] = np.broadcast_to(a["sgu_ln_b_2"], (P, D))
    sgt[:, 2 * D:2 * D + SGU_G * P] = np.broadcast_to(a["b_spatial_2"].reshape(-1), (P, SGU_G * P))
    sgt[:, 2 * D + SGU_G * P:] = a["w_spatial_2"].transpose(2, 0, 1).reshape(P, SGU_G * P)
    xt = np.ascontiguousarray(a["x"][0].T.reshape(KT, P, T).transpose(1, 0, 2))
    arrays = {"w": W, "x": xt, "const": constants(), "par_l": parl, "par_s": pars,
              "rope1": rope_tables(500000.0, ROT, HD), "rope2": rope_tables(10000.0, DK, DK),
              "sgu_tables": sgt, "distances": distances()}

    strides = {}
    for _ in range(2):
        nc = bacc.Bacc("TRN2", target_bir_lowering=False, num_devices=1)
        args = [nc.dram_tensor(f"in_{n}_dram", v.shape, F32, kind="ExternalInput").ap() for n, v in arrays.items()]
        args.append(nc.dram_tensor("out_0_dram", (P, KT, T), F32, kind="ExternalOutput").ap())
        program(nc, *args, strides)
    r = run(nc, [{f"in_{n}_dram": v for n, v in arrays.items()}], core_ids=[0])
    got = r.results[0]["out_0_dram"]
    return np.ascontiguousarray(got.transpose(2, 1, 0).reshape(1, T, D))
```
